# Optimizing a Trainium2 kernel written in Bass

```python
import jax, jax.numpy as jnp
from jax import lax
import numpy as np

D_MODEL = 1024
BATCH = 1
SEQ = 512
DEPTH = 2

N_MIXERS = 4
HEAD_DIM = 64
N_HEADS = D_MODEL // HEAD_DIM
SWA_KV_HEADS = 4
SWA_WINDOW = 128
SWA_BLOCK = 128
NSA_KV_GROUPS = 2
NSA_CMP_LEN = 32
NSA_CMP_STRIDE = 16
NSA_SEL_LEN = 64
NSA_TOPK = 8
NSA_WINDOW = 512
NSA_QBLOCK = 64
NSA_FORCE_BONUS = 1.0e4
GLA_HEADS = 4
GLA_DK = D_MODEL // 2
GLA_DV = D_MODEL
GLA_GATE_RANK = 16
GLA_TAU = 16.0
GLA_CHUNK = 64
POOL_WINDOWS = (2, 4, 8, 16)
POOL_GROUP = D_MODEL // 4
MEM_LEN = 256
XATTN_HEADS = 4
FFN_DIM = 2816
DN_ALPHA = (2 * DEPTH) ** 0.25
DN_BETA = (8 * DEPTH) ** -0.25
LN_EPS = 1e-5
NEG_INF = -1e30

SWA_IN = N_HEADS * HEAD_DIM + 2 * SWA_KV_HEADS * HEAD_DIM
NSA_IN = N_HEADS * HEAD_DIM + 6 * NSA_KV_GROUPS * HEAD_DIM + 3 * N_HEADS
GLA_IN = 2 * GLA_DK + 2 * GLA_DV + GLA_GATE_RANK

kernel_name = 'hybrid_interleaved_deepnorm_macaron_block'

def layer_norm(x, g, b):
    xf = x.astype(jnp.float32)
    mu = jnp.mean(xf, -1, keepdims=True)
    var = jnp.mean(jnp.square(xf - mu), -1, keepdims=True)
    return ((xf - mu) * lax.rsqrt(var + LN_EPS) * g + b).astype(x.dtype)

def alibi_slopes(n):
    return jnp.exp2(-8.0 * jnp.arange(1, n + 1, dtype=jnp.float32) / n)

def swiglu(x, w_gate, w_up, w_down):
    return (jax.nn.silu(x @ w_gate) * (x @ w_up)) @ w_down

def swa_mixer(x, w_in, sinks, w_out):
    B, S, _ = x.shape
    H, G, d, L = N_HEADS, SWA_KV_HEADS, HEAD_DIM, SWA_BLOCK
    R = H // G
    nb = S // L
    q, k, v = jnp.split(x @ w_in, [H * d, H * d + G * d], axis=-1)
    q = q.reshape(B, nb, L, G, R, d) * d ** -0.5
    k = k.reshape(B, nb, L, G, d)
    v = v.reshape(B, nb, L, G, d)
    prev = lambda t: jnp.concatenate([jnp.zeros_like(t[:, :1]), t[:, :-1]], axis=1)
    kb = jnp.concatenate([prev(k), k], axis=2)
    vb = jnp.concatenate([prev(v), v], axis=2)
    q_abs = jnp.arange(nb)[:, None] * L + jnp.arange(L)[None, :]
    k_abs = jnp.arange(nb)[:, None] * L - L + jnp.arange(2 * L)[None, :]
    dist = q_abs[:, :, None] - k_abs[:, None, :]
    valid = (dist >= 0) & (dist < SWA_WINDOW) & (k_abs[:, None, :] >= 0)
    slopes = alibi_slopes(H).reshape(1, G, R, 1, 1)
    s = jnp.einsum('bnqgrd,bnkgd->bngrqk', q, kb).astype(jnp.float32)
    s = s - slopes * dist[:, None, None].astype(jnp.float32)
    s = jnp.where(valid[:, None, None], s, NEG_INF)
    sink = sinks.astype(jnp.float32).reshape(1, 1, G, R, 1, 1)
    m = jnp.maximum(jnp.max(s, -1, keepdims=True), sink)
    e = jnp.exp(s - m)
    p = e / (jnp.sum(e, -1, keepdims=True) + jnp.exp(sink - m))
    o = jnp.einsum('bngrqk,bnkgd->bnqgrd', p.astype(v.dtype), vb)
    return o.reshape(B, S, H * d) @ w_out

def nsa_mixer(x, w_in, cmp_pos, cmp_w1, cmp_w2, w_out):
    B, S, _ = x.shape
    H, G, d = N_HEADS, NSA_KV_GROUPS, HEAD_DIM
    R = H // G
    L, STR, SL, W, QB = NSA_CMP_LEN, NSA_CMP_STRIDE, NSA_SEL_LEN, NSA_WINDOW, NSA_QBLOCK
    n_cmp = S // STR - 1
    n_sel = S // SL
    topk = min(NSA_TOPK, n_sel)
    f32 = jnp.float32
    splits = [H * d + i * G * d for i in range(7)]
    q, kc, vc, ks, vs, kw, vw, gl = jnp.split(x @ w_in, splits, axis=-1)
    q = q.reshape(B, S, G, R, d) * d ** -0.5
    kv = lambda t: t.reshape(B, S, G, d)
    slopes = alibi_slopes(H).reshape(G, R)
    t_pos = jnp.arange(S)

    def compress(t, pos, w1, w2):
        c = t.reshape(B, S // STR, STR, G, d)
        blocks = jnp.concatenate([c[:, :-1], c[:, 1:]], axis=2) + pos[:, None, :]
        return jax.nn.gelu(jnp.einsum('bnlgd,lde->bnge', blocks, w1)) @ w2

    k_cmp = compress(kv(kc), cmp_pos[0], cmp_w1[0], cmp_w2[0])
    v_cmp = compress(kv(vc), cmp_pos[1], cmp_w1[1], cmp_w2[1])
    blk = jnp.arange(n_cmp) * STR
    dist_c = (t_pos[:, None] - (blk[None, :] + (L - 1) / 2)).astype(f32)
    valid_c = (blk[None, :] + L - 1) <= t_pos[:, None]
    s_c = jnp.einsum('bsgrd,bngd->bgrsn', q, k_cmp).astype(f32) - slopes[:, :, None, None] * dist_c
    p_c = jnp.where(valid_c, jax.nn.softmax(jnp.where(valid_c, s_c, NEG_INF), axis=-1), 0.0)
    o_cmp = jnp.einsum('bgrsn,bngd->bsgrd', p_c.astype(x.dtype), v_cmp)

    sel_start = jnp.arange(n_sel) * SL
    overlap = ((blk[:, None] < sel_start[None, :] + SL) & (blk[:, None] + L > sel_start[None, :])).astype(f32)
    imp = jnp.einsum('bgrsn,nm->bgsm', p_c, overlap)
    cur = t_pos // SL
    j = jnp.arange(n_sel)
    causal_sel = j[None, :] <= cur[:, None]
    forced = (j[None, :] == 0) | (j[None, :] == cur[:, None]) | (j[None, :] == cur[:, None] - 1)
    score = jnp.where(causal_sel, imp + jnp.where(forced, NSA_FORCE_BONUS, 0.0), NEG_INF)
    top_score, sel_idx = lax.top_k(score, topk)
    sel_ok = top_score > 0.5 * NEG_INF

    ks_blocks = kv(ks).reshape(B, n_sel, SL, G, d).transpose(0, 3, 1, 2, 4)
    vs_blocks = kv(vs).reshape(B, n_sel, SL, G, d).transpose(0, 3, 1, 2, 4)
    kw_pad = jnp.pad(kv(kw), ((0, 0), (W, 0), (0, 0), (0, 0)))
    vw_pad = jnp.pad(kv(vw), ((0, 0), (W, 0), (0, 0), (0, 0)))
    b_ix = jnp.arange(B)[:, None, None, None]
    g_ix = jnp.arange(G)[None, :, None, None]

    def query_block(c):
        q0 = c * QB
        qc = lax.dynamic_slice_in_dim(q, q0, QB, axis=1)
        tq = q0 + jnp.arange(QB)
        idx = lax.dynamic_slice_in_dim(sel_idx, q0, QB, axis=2)
        ok = lax.dynamic_slice_in_dim(sel_ok, q0, QB, axis=2)
        k_sel = ks_blocks[b_ix, g_ix, idx]
        v_sel = vs_blocks[b_ix, g_ix, idx]
        kpos = idx[..., None] * SL + jnp.arange(SL)
        dsel = tq[None, None, :, None, None] - kpos
        msel = ok[..., None] & (dsel >= 0)
        s = jnp.einsum('bqgrd,bgqkld->bgrqkl', qc, k_sel).astype(f32)
        s = s - slopes[None, :, :, None, None, None] * dsel[:, :, None].astype(f32)
        s = jnp.where(msel[:, :, None], s, NEG_INF).reshape(B, G, R, QB, topk * SL)
        p = jax.nn.softmax(s, axis=-1).reshape(B, G, R, QB, topk, SL).astype(x.dtype)
        o_sel = jnp.einsum('bgrqkl,bgqkld->bqgrd', p, v_sel)
        kwin = lax.dynamic_slice_in_dim(kw_pad, q0, W + QB, axis=1)
        vwin = lax.dynamic_slice_in_dim(vw_pad, q0, W + QB, axis=1)
        wpos = q0 - W + jnp.arange(W + QB)
        dw = tq[:, None] - wpos[None, :]
        mw = (dw >= 0) & (dw < W) & (wpos[None, :] >= 0)
        sw = jnp.einsum('bqgrd,bkgd->bgrqk', qc, kwin).astype(f32) - slopes[:, :, None, None] * dw.astype(f32)
        pw = jax.nn.softmax(jnp.where(mw, sw, NEG_INF), axis=-1).astype(x.dtype)
        o_win = jnp.einsum('bgrqk,bkgd->bqgrd', pw, vwin)
        return o_sel, o_win

    o_sel, o_win = lax.map(query_block, jnp.arange(S // QB))
    o_sel = jnp.moveaxis(o_sel, 0, 1).reshape(B, S, G, R, d)
    o_win = jnp.moveaxis(o_win, 0, 1).reshape(B, S, G, R, d)
    g = jax.nn.sigmoid(gl.astype(f32)).reshape(B, S, 3, G, R)[..., None]
    o = g[:, :, 0] * o_cmp + g[:, :, 1] * o_sel + g[:, :, 2] * o_win
    return o.astype(x.dtype).reshape(B, S, H * d) @ w_out

def gla_mixer(x, w_in, w_gate2, b_gate, norm_g, w_out):
    B, S, _ = x.shape
    H, C = GLA_HEADS, GLA_CHUNK
    dk, dv = GLA_DK // H, GLA_DV // H
    nc = S // C
    f32 = jnp.float32
    q, k, v, g_lr, r = jnp.split(
        x @ w_in, [GLA_DK, 2 * GLA_DK, 2 * GLA_DK + GLA_DV, 2 * GLA_DK + GLA_DV + GLA_GATE_RANK], axis=-1)
    log_a = jax.nn.log_sigmoid((g_lr @ w_gate2 + b_gate).astype(f32)) / GLA_TAU

    def chunks(t, hd):
        return t.astype(f32).reshape(B, nc, C, H, hd).transpose(1, 0, 3, 2, 4)

    qc = chunks(q, dk) * dk ** -0.5
    kc = chunks(k, dk)
    vc = chunks(v, dv)
    bc = jnp.cumsum(chunks(log_a, dk), axis=3)
    causal = jnp.tril(jnp.ones((C, C), dtype=bool))

    def step(state, inp):
        q_, k_, v_, b_ = inp
        decay = jnp.exp(jnp.where(causal[:, :, None], b_[:, :, :, None, :] - b_[:, :, None, :, :], NEG_INF))
        att = jnp.einsum('bhik,bhjk,bhijk->bhij', q_, k_, decay)
        out = jnp.einsum('bhij,bhjv->bhiv', att, v_) + jnp.einsum('bhik,bhkv->bhiv', q_ * jnp.exp(b_), state)
        b_last = b_[:, :, -1, :]
        state = jnp.exp(b_last)[..., None] * state + jnp.einsum(
            'bhjk,bhjv->bhkv', k_ * jnp.exp(b_last[:, :, None, :] - b_), v_)
        return state, out

    state0 = jnp.zeros((B, H, dk, dv), f32)
    _, o = lax.scan(step, state0, (qc, kc, vc, bc))
    o = o.transpose(1, 0, 3, 2, 4).reshape(B, S, H, dv)
    o = o * lax.rsqrt(jnp.mean(jnp.square(o), -1, keepdims=True) + LN_EPS) * norm_g
    o = o.reshape(B, S, GLA_DV) * jax.nn.silu(r.astype(f32))
    return o.astype(x.dtype) @ w_out

def pool_mixer(x, w_grp, scale):
    B, S, D = x.shape
    ng = len(POOL_WINDOWS)
    xg = x.astype(jnp.float32).reshape(B, S, ng, POOL_GROUP)
    csum = jnp.pad(jnp.cumsum(xg, axis=1), ((0, 0), (1, 0), (0, 0), (0, 0)))
    t = jnp.arange(S)
    pooled = []
    for gi, w in enumerate(POOL_WINDOWS):
        lo = jnp.maximum(t + 1 - w, 0)
        cg = csum[:, :, gi]
        total = cg[:, 1:] - cg[:, lo]
        pooled.append(total / (t + 1 - lo).astype(jnp.float32)[:, None])
    pooled = jnp.stack(pooled, axis=2)
    y = jnp.einsum('bsgc,gce->bsge', pooled - xg, w_grp.astype(jnp.float32)).reshape(B, S, D) * scale
    return y.astype(x.dtype)

def mem_cross_attention(x, mem, w_q, w_kv, w_o):
    B, S, D = x.shape
    M = mem.shape[1]
    Hx = XATTN_HEADS
    dh = D // Hx
    q = (x @ w_q).reshape(B, S, Hx, dh) * dh ** -0.5
    k, v = jnp.split(mem @ w_kv, 2, axis=-1)
    k = k.reshape(B, M, Hx, dh)
    v = v.reshape(B, M, Hx, dh)
    s = jnp.einsum('bshd,bmhd->bhsm', q, k).astype(jnp.float32)
    p = jax.nn.softmax(s, axis=-1).astype(v.dtype)
    o = jnp.einsum('bhsm,bmhd->bshd', p, v).reshape(B, S, D)
    return o @ w_o

def setup_inputs(seed: int = 0) -> dict:
    key = jax.random.key(seed)
    keys = jax.random.split(key, 28)
    D, F, d, H = D_MODEL, FFN_DIM, HEAD_DIM, N_HEADS
    nA, nB, nC, nD = [len(range(k, DEPTH, N_MIXERS)) for k in range(N_MIXERS)]
    L = NSA_CMP_LEN

    def nrm(i, shape, scale):
        return scale * jax.random.normal(keys[i], shape, jnp.float32)

    return {
        'x': nrm(0, (BATCH, SEQ, D), 1.0),
        'mem': nrm(1, (BATCH, MEM_LEN, D), 1.0),
        'ln_g': jnp.ones((DEPTH, 4, D), jnp.float32) + nrm(2, (DEPTH, 4, D), 0.02),
        'ln_b': nrm(3, (DEPTH, 4, D), 0.02),
        'ffn1_w_gate': nrm(4, (DEPTH, D, F), D ** -0.5),
        'ffn1_w_up': nrm(5, (DEPTH, D, F), D ** -0.5),
        'ffn1_w_down': nrm(6, (DEPTH, F, D), DN_BETA * F ** -0.5),
        'ffn2_w_gate': nrm(7, (DEPTH, D, F), D ** -0.5),
        'ffn2_w_up': nrm(8, (DEPTH, D, F), D ** -0.5),
        'ffn2_w_down': nrm(9, (DEPTH, F, D), DN_BETA * F ** -0.5),
        'xattn_w_q': nrm(10, (DEPTH, D, D), D ** -0.5),
        'xattn_w_kv': nrm(11, (DEPTH, D, 2 * D), D ** -0.5),
        'xattn_w_o': nrm(12, (DEPTH, D, D), DN_BETA * D ** -0.5),
        'swa_w_in': nrm(13, (nA, D, SWA_IN), D ** -0.5),
        'swa_sinks': nrm(14, (nA, H), 1.0),
        'swa_w_out': nrm(15, (nA, H * d, D), DN_BETA * D ** -0.5),
        'nsa_w_in': nrm(16, (nB, D, NSA_IN), D ** -0.5),
        'nsa_cmp_pos': nrm(17, (nB, 2, L, d), 0.1),
        'nsa_cmp_w1': nrm(18, (nB, 2, L, d, d), (L * d) ** -0.5),
        'nsa_cmp_w2': nrm(19, (nB, 2, d, d), d ** -0.5),
        'nsa_w_out': nrm(20, (nB, H * d, D), DN_BETA * D ** -0.5),
        'gla_w_in': nrm(21, (nC, D, GLA_IN), D ** -0.5),
        'gla_w_gate2': nrm(22, (nC, GLA_GATE_RANK, GLA_DK), GLA_GATE_RANK ** -0.5),
        'gla_b_gate': nrm(23, (nC, GLA_DK), 0.1),
        'gla_norm_g': jnp.ones((nC, GLA_DV // GLA_HEADS), jnp.float32) + nrm(24, (nC, GLA_DV // GLA_HEADS), 0.02),
        'gla_w_out': nrm(25, (nC, GLA_DV, D), DN_BETA * GLA_DV ** -0.5),
        'pool_w': nrm(26, (nD, len(POOL_WINDOWS), POOL_GROUP, POOL_GROUP), DN_BETA * POOL_GROUP ** -0.5),
        'pool_scale': jnp.ones((nD, D), jnp.float32) + nrm(27, (nD, D), 0.02),
    }

def reference(x, mem, ln_g, ln_b,
              ffn1_w_gate, ffn1_w_up, ffn1_w_down, ffn2_w_gate, ffn2_w_up, ffn2_w_down,
              xattn_w_q, xattn_w_kv, xattn_w_o,
              swa_w_in, swa_sinks, swa_w_out,
              nsa_w_in, nsa_cmp_pos, nsa_cmp_w1, nsa_cmp_w2, nsa_w_out,
              gla_w_in, gla_w_gate2, gla_b_gate, gla_norm_g, gla_w_out,
              pool_w, pool_scale):
    for i in range(DEPTH):
        kind = i % N_MIXERS
        j = i // N_MIXERS
        x = layer_norm(DN_ALPHA * x + 0.5 * swiglu(x, ffn1_w_gate[i], ffn1_w_up[i], ffn1_w_down[i]),
                       ln_g[i, 0], ln_b[i, 0])
        if kind == 0:
            y = swa_mixer(x, swa_w_in[j], swa_sinks[j], swa_w_out[j])
        elif kind == 1:
            y = nsa_mixer(x, nsa_w_in[j], nsa_cmp_pos[j], nsa_cmp_w1[j], nsa_cmp_w2[j], nsa_w_out[j])
        elif kind == 2:
            y = gla_mixer(x, gla_w_in[j], gla_w_gate2[j], gla_b_gate[j], gla_norm_g[j], gla_w_out[j])
        else:
            y = pool_mixer(x, pool_w[j], pool_scale[j])
        x = layer_norm(DN_ALPHA * x + y, ln_g[i, 1], ln_b[i, 1])
        x = layer_norm(DN_ALPHA * x + mem_cross_attention(x, mem, xattn_w_q[i], xattn_w_kv[i], xattn_w_o[i]),
                       ln_g[i, 2], ln_b[i, 2])
        x = layer_norm(DN_ALPHA * x + 0.5 * swiglu(x, ffn2_w_gate[i], ffn2_w_up[i], ffn2_w_down[i]),
                       ln_g[i, 3], ln_b[i, 3])
    return x


_drawn_inputs = setup_inputs


def setup_inputs(seed=0):
    import zlib

    import numpy as np

    out = dict(_drawn_inputs(seed))
    spreads = {}
    factors = {'swa_sinks': 2.918, 'nsa_cmp_pos': 5.17}
    for name, (base, spread) in spreads.items():
        noise = np.random.default_rng([zlib.crc32(name.encode()), seed]).standard_normal(out[name].shape)
        drawn = base * np.exp(spread * noise) if base else spread * noise
        out[name] = __import__('jax').numpy.asarray(drawn.astype(out[name].dtype))
    for name, factor in factors.items():
        out[name] = (out[name] * factor).astype(out[name].dtype)
    return out
```

```python
from contextlib import ExitStack

import numpy as np
import concourse.bass as bass
from concourse import mybir

ALU = mybir.AluOpType
ACT = mybir.ActivationFunctionType
AX = mybir.AxisListType
F32 = mybir.dt.float32
F32R = mybir.dt.float32r
I32 = mybir.dt.int32

P = 128
D = 1024
KC = D // P
SEQ = 512
NT = SEQ // P
MEM = 256
MT = MEM // P
DEPTH = 2
HEADS = 16
FFN = 2816
FPARTS = (8, 7, 7)
NCMP = SEQ // 16 - 1
CL = 32
EPS = 1e-5
ALPHA = (2 * DEPTH) ** 0.25
MASKED = -1.0e34
SLOTS = 4
SLAB = KC * P
NLN = 4 * DEPTH
MEM_FILL = {0: (0, 0, 8), 1: (0, 8, 8), 2: (1, 0, 4), 3: (1, 4, 4), 4: (1, 8, 4), 5: (1, 12, 4)}
FILL_BANKS = (6, 7, 2, 3)

assert sum(FPARTS) * P == FFN


class Stage:

    def __init__(self, kind, s0, n, x=None, part=None, nf=None, h0=None, w=None, ln=None, first=None, last=None,
                 of=None):
        self.kind, self.s0, self.n, self.x, self.part, self.nf, self.h0 = kind, s0, n, x, part, nf, h0
        self.w, self.ln, self.first, self.last, self.of = w, ln, first, last, of
        self.id = self.sem = None


class Unit:

    def __init__(self, u, b, half, head, br, i, keys, g, first, last):
        self.u, self.b, self.half, self.head, self.br = u, b, half, head, br
        self.i, self.keys, self.g, self.first, self.last = i, keys, g, first, last


class Group:

    def __init__(self, g, br, b, half, head, first):
        self.g, self.br, self.b, self.half, self.head, self.first = g, br, b, half, head, first
        self.last = first


class Block:

    def __init__(self, b, first):
        self.b, self.first, self.last, self.groups = b, first, first, 0


class Turn:

    def __init__(self, kind):
        self.kind, self.units, self.groups, self.blocks = kind, [], [], []
        self.heads = self.n = self.ng = self.nb = 0


def head_pairs(kind):
    if kind == "swa":
        return [(i, i + 4) if e == 0 else (8 + i, 12 + i) for i in range(4) for e in range(2)]
    return [(c, c + 8) for c in range(8)]


def plan():
    stages, chunks = [], []

    def stage(kind, sizes, **more):
        stages.append(Stage(kind, len(chunks), len(sizes), **more))
        chunks.extend(sizes)

    def memory(ln):
        if ln in MEM_FILL:
            layer, c0, n = MEM_FILL[ln]
            stage("mem", [KC] * n, h0=c0, w=(layer, 0), ln=ln)

    ln = 0

    def ffn(layer, which, ln):
        for part, nf in enumerate(FPARTS):
            h0 = sum(FPARTS[:part])
            stage("up", [KC] * (2 * nf), x=ln, part=part, nf=nf, h0=h0, w=(layer, which))
            stage("out", [nf] * KC, part=part, nf=nf, h0=h0, ln=ln, w=(layer, which),
                  first=part == 0, last=part == len(FPARTS) - 1, of="ffn")
        memory(ln)

    for layer in range(DEPTH):
        ffn(layer, 1, ln)
        ln += 1
        kind = "swa" if layer == 0 else "nsa"
        stage("kv_" + kind, [KC] * (4 if kind == "swa" else 7), x=ln)
        stage("att_" + kind, [KC] * KC, x=ln)
        stage("out", [KC] * KC, part=0, nf=KC, ln=ln, first=True, last=True, of=kind, w=(layer, 0))
        memory(ln)
        ln += 1
        stage("att_x", [KC] * KC, x=ln, w=(layer, 0))
        stage("out", [KC] * KC, part=0, nf=KC, ln=ln, first=True, last=True, of="x", w=(layer, 0))
        memory(ln)
        ln += 1
        ffn(layer, 2, ln)
        ln += 1
    return stages, chunks


def attention_units(kind):
    T = Turn(kind)
    nblocks = 2 if kind == "x" else 4
    for b in range(nblocks):
        block = Block(b, len(T.units))
        for half in ((0,) if kind == "x" else (0, 1)):
            head = b if kind == "x" else 2 * b + half
            for br in (("cmp", "sel", "win") if kind == "nsa" else (kind,)):
                if br == "cmp":
                    tiles = [(0, None)]
                elif br in ("sel", "win"):
                    tiles = [(i, list(range(i + 1))) for i in range(NT)]
                elif br == "swa":
                    tiles = [(i, [k for k in (i - 1, i) if k >= 0]) for i in range(NT)]
                else:
                    tiles = [(i, list(range(MT))) for i in range(NT)]
                for n, (i, keys) in enumerate(tiles):
                    if n == 0 or kind == "x":
                        T.groups.append(Group(g=len(T.groups), br=br, b=b, half=half, head=head,
                                                        first=len(T.units)))
                    g = T.groups[-1]
                    g.last = len(T.units)
                    T.units.append(Unit(u=len(T.units), b=b, half=half, head=head, br=br, i=i,
                                                   keys=keys, g=g.g, first=n == 0, last=n == len(tiles) - 1))
        block.last = len(T.units) - 1
        block.groups = len(T.groups)
        T.blocks.append(block)
    T.heads = nblocks if kind == "x" else 2 * nblocks
    T.n, T.ng, T.nb = len(T.units), len(T.groups), nblocks
    return T


def build(nc, io):
    stages, chunks = plan()
    total = len(chunks)

    with ExitStack() as ctx:
        def sb(name, shape, dt=F32):
            return ctx.enter_context(nc.sbuf_tensor(name, shape, dt))

        def sem(name):
            return ctx.enter_context(nc.semaphore(name))

        x = sb("x", [P, KC, SEQ])
        x_hi = sb("x_hi", [P, KC, SEQ], F32R)
        x_lo = sb("x_lo", [P, KC, SEQ], F32R)
        h_hi = sb("h_hi", [P, 12, SEQ], F32R)
        h_lo = sb("h_lo", [P, 12, SEQ], F32R)
        w_raw = [sb(f"w_raw{i}", [P, SLAB]) for i in range(SLOTS)]
        w_hi = [sb(f"w_hi{i}", [P, SLAB], F32R) for i in range(SLOTS)]
        w_lo = [sb(f"w_lo{i}", [P, SLAB], F32R) for i in range(SLOTS)]
        mem_hi = h_hi[:, 8:12, :].rearrange("p a b -> p (a b)").rearrange("p (k m) -> p k m", k=KC)
        mem_lo = h_lo[:, 8:12, :].rearrange("p a b -> p (a b)").rearrange("p (k m) -> p k m", k=KC)

        kvs = sb("kvs", [P, 3264])
        mem_kv = sb("mem_kv", [P, 2 * MT * D])
        keysT = kvs[:, 0:2048].rearrange("p (n t) -> p n t", n=4)
        vals = kvs[:, 2048:3072].rearrange("p (n i d) -> p n i d", n=2, i=NT)
        kcmpT = kvs[:, 3072:3072 + NCMP]
        vcmp = kvs[0:NCMP, 3136:3136 + P]
        memkT = mem_kv[:, 0:KC * MEM].rearrange("p (c m) -> p c m", c=KC)
        memv = mem_kv[:, KC * MEM:].rearrange("p (i d) -> p i d", i=MT)
        mem_raw = kvs[:, 0:2048].rearrange("p (k m) -> p k m", k=KC)

        wk = sb("wk", [P, 7168])
        gated = [wk[:, 512 * i:512 * (i + 1)] for i in range(2)]
        hidden = [wk[:, 1024 + 512 * i:1024 + 512 * (i + 1)] for i in range(2)]
        ysum = wk[:, 2048:2560]
        std = wk[:, 2560:3072]
        rstd = wk[:, 3072:3584]
        square = [wk[:, 3584 + 512 * i:3584 + 512 * (i + 1)] for i in range(4)]
        biasb = [wk[:, 640 * i:640 * (i + 1)] for i in range(2)]
        sS = [wk[:, 1280 + 512 * i:1280 + 512 * (i + 1)] for i in range(2)]
        prob = [wk[:, (2304, 2816, 6656)[i]:(2304, 2816, 6656)[i] + 512] for i in range(3)]
        probT = [wk[:, 3328 + 512 * i:3328 + 512 * (i + 1)] for i in range(2)]
        otmp = wk[:, 6400:6656]
        qs_mix = [wk[:, 4352 + 512 * i:4352 + 512 * (i + 1)].rearrange("p (c t) -> p c t", c=1) for i in range(2)]
        otok_mix = [wk[:, 5376 + 512 * i:5376 + 512 * (i + 1)] for i in range(2)]
        qs_mem = [kvs[:, 1024 * i:1024 * (i + 1)].rearrange("p (c t) -> p c t", c=2) for i in range(2)]
        otok_mem = [kvs[:, 2048:3072], wk[:, 4352:5376]]
        cw1 = wk[:, 0:4096].rearrange("p (n l e) -> p n l e", n=2, l=CL)
        cblk = [wk[:, 4096 + 992 * i:4096 + 992 * (i + 1)].rearrange("p (l n) -> p l n", l=CL) for i in range(2)]
        cpos = wk[:, 6144:6208].rearrange("p (n l) -> p n l", n=2)
        cw2 = wk[:, 6208:6336].rearrange("p (n e) -> p n e", n=2)
        ch1 = [wk[:, 6336 + 32 * i:6336 + 32 * i + NCMP] for i in range(2)]

        lng = sb("lng", [P, NLN, KC])
        lnb = sb("lnb", [P, NLN, KC])
        ones = sb("ones", [P, P])
        ident = sb("ident", [P, P])
        slope_swa = sb("slope_swa", [P, HEADS])
        slope_nsa = sb("slope_nsa", [P, HEADS])
        sinks = sb("sinks", [P, HEADS])
        dist_i = mem_kv[:, 0:896].bitcast(I32)
        dist = sb("dist", [P, 896])
        eps = sb("eps", [P, 1])
        gates = sb("gates", [P, NT, 48])
        small = sb("small", [P, 112])
        negm = small[:, 0:16]
        sinkexp = small[:, 32:48]
        tot = small[:, 48:52]
        rinv = small[:, 52:56]
        rgate = small[:, 56:60]
        rowmax = small[:, 60:76]
        cmpmax = small[:, 76:80]
        sums = small[:, 80:112]

        bank = [ctx.enter_context(nc.psum_tensor(f"bank{i}", [P, 512], F32)) for i in range(8)]
        B_OT, B_PV, B_S, B_T, B_MU, B_VAR = 1, 2, 4, 6, 4, 5

        raw_landed = [sem(f"raw_landed{i}") for i in range(SLOTS)]
        hi_ready = sem("hi_ready")
        lo_ready = sem("lo_ready")
        slab_done = sem("slab_done")
        x_ready = [sem(f"x_ready{n}") for n in range(NLN)]
        x_in = sem("x_in")
        cleared = sem("cleared")
        x_hi0 = sem("x_hi0")
        consts_in = sem("consts_in")
        pool_set = sem("pool_set")
        iota_done = sem("iota_done")
        dist_f = sem("dist_f")
        dist_ready = sem("dist_ready")
        mem_in = sem("mem_in")
        mem_rounded = sem("mem_rounded")
        mem_split = sem("mem_split")
        mem_evac = sem("mem_evac")
        cmp_in = sem("cmp_in")
        out_done = sem("out_done")
        ln = {k: sem("ln_" + k) for k in ("sum", "mu", "dev", "sq", "var", "std", "rstd", "norm", "xf")}
        for n, st in enumerate(stages):
            st.id = n
            if st.kind in ("up", "out") and st.part:
                st.sem = stages[n - 2].sem
                continue
            if st.kind == "up":
                names = ("gated", "hidden", "hhi", "hlo")
            elif st.kind == "out":
                names = ("free",)
            elif st.kind.startswith("kv"):
                names = ("aevac", "devac", "gexp", "gadd", "gate", "blkk", "c1", "c1g", "c2", "c2e")
                if st.kind == "kv_swa":
                    names = names[:2]
            elif st.kind == "mem":
                names = ()
            else:
                names = ("q", "s", "add", "nm", "p", "t", "pt", "pv", "fin", "chain", "ot", "ohi", "olo")
                names += {"att_x": (), "att_swa": ("bias", "sink"), "att_nsa": ("bias", "csum")}[st.kind]
            st.sem = {k: sem(f"{k}_{n}") for k in names}
        final = stages[-1]

        def fill_banks(st):
            return sum(m.n // 2 for m in stages[:st.id] if m.kind == "mem")

        def prior(st, kind=None):
            return next(s for s in reversed(stages[:st.id]) if kind is None or s.kind == kind)

        block = ctx.enter_context(nc.Block())

        def raw_count(base, i):
            return 16 * (base // SLOTS + 1) + 16 * i

        @block.sync
        def _(sp):
            def load(base, i, src):
                if base >= SLOTS:
                    sp.wait_ge(lo_ready, base - SLOTS + 1 + SLOTS * i)
                slot = base % SLOTS
                sp.dma_start(w_raw[slot][:, 0:src.shape[-1]], src).then_inc(raw_landed[slot], 16)

            runs = []
            at = {7: 0, 8: 0}
            for s, n in enumerate(chunks):
                if s < SLOTS or s == SLOTS or runs[-1][2] != n:
                    runs.append([s, 0, n, at[n]])
                runs[-1][1] += 1
                at[n] += 1
            for s0, count, n, row in runs:
                w = io["w%d" % n]
                turns = count // SLOTS
                if turns > 1:
                    with sp.Fori(0, turns) as i:
                        for k in range(SLOTS):
                            load(s0 + k, i, w[bass.ds(row + k + SLOTS * i, 1), :, :].rearrange("a p n -> (a p) n"))
                else:
                    turns = 0
                for k in range(SLOTS * turns, count):
                    load(s0 + k, 0, w[row + k, :, :])
            for j in range(KC):
                sp.wait_ge(ln["xf"], KC * final.ln + j + 1)
                sp.dma_start(io["out"][:, j, :], x[:, j, :]).then_inc(out_done, 16)
            sp.wait_ge(out_done, 16 * KC)

        @block.gpsimd
        def _(pool):
            pool.memset(ident[:], 0.0).then_inc(pool_set, 1)
            pool.memset(ones[:], 1.0 / D).then_inc(pool_set, 1)
            pool.memset(eps[:], EPS).then_inc(pool_set, 1)
            for kind, table in (("swa", slope_swa), ("nsa", slope_nsa)):
                for c, pair in enumerate(head_pairs(kind)):
                    for half in range(2):
                        pool.memset(table[:, 2 * c + half:2 * c + half + 1],
                                    float(2.0 ** (-8.0 * (pair[half] + 1) / HEADS))).then_inc(pool_set, 1)
            pool.iota(dist_i[:, 0:512], [[1, 512]], base=-384, channel_multiplier=-1).then_inc(iota_done, 1)
            pool.iota(dist_i[:, 512:640].rearrange("p (i n) -> p i n", i=NT), [[-128, NT], [16, 32]], base=0,
                      channel_multiplier=-1).then_inc(iota_done, 1)
            pool.iota(dist_i[:, 640:896], [[1, 256]], base=-128, channel_multiplier=-1).then_inc(iota_done, 1)
            pool.wait_ge(pool_set, 3)
            pool.affine_select(out=ident[:], in_=ident[:], compare_op=ALU.not_equal, fill=1.0, base=0,
                               pattern=[[-1, P]], channel_multiplier=1).then_inc(pool_set, 1)
            pool.wait_ge(dist_f, 3)
            pool.affine_select(out=dist[:, 0:512], in_=dist[:, 0:512], compare_op=ALU.is_ge, fill=MASKED, base=384,
                               pattern=[[-1, 512]], channel_multiplier=1).then_inc(dist_ready, 1)
            cd = dist[:, 512:640].rearrange("p (i n) -> p i n", i=NT)
            pool.affine_select(out=cd, in_=cd, compare_op=ALU.is_ge, fill=MASKED, base=-31,
                               pattern=[[128, NT], [-16, 32]], channel_multiplier=1).then_inc(dist_ready, 1)
            pool.affine_select(out=dist[:, 640:896], in_=dist[:, 640:896], compare_op=ALU.is_ge, fill=MASKED,
                               base=128, pattern=[[-1, 256]], channel_multiplier=1).then_inc(dist_ready, 1)
            pool.wait_ge(dist_ready, 3)
            pool.affine_select(out=dist[:, 640:896], in_=dist[:, 640:896], compare_op=ALU.is_ge, fill=MASKED,
                               base=-1, pattern=[[1, 256]], channel_multiplier=-1).then_inc(dist_ready, 1)

            def split(base, i, n):
                slot = base % SLOTS
                pool.wait_ge(hi_ready, base + 1 + SLOTS * i)
                pool.tensor_tensor(w_lo[slot][:, 0:n * P], w_raw[slot][:, 0:n * P],
                                   w_hi[slot][:, 0:n * P].bitcast(F32), ALU.subtract).then_inc(lo_ready, 1)

            s = 0
            while s < total:
                n = chunks[s]
                count = next((e for e in range(s, total) if chunks[e] != n), total) - s
                turns = count // SLOTS
                if turns:
                    with pool.Fori(0, turns) as i:
                        for k in range(SLOTS):
                            split(s + k, i, n)
                for k in range(SLOTS * turns, count):
                    split(s + k, 0, n)
                s += count

        @block.scalar
        def _(act):
            def round_slab(base, i=0):
                if base >= total:
                    return
                slot = base % SLOTS
                act.wait_ge(raw_landed[slot], raw_count(base, i))
                if base >= SLOTS:
                    act.wait_ge(slab_done, base - SLOTS + 1 + SLOTS * i)
                act.activation(w_hi[slot][:], w_raw[slot][:], ACT.Copy).then_inc(hi_ready, 1)

            act.dma_start(x[:], io["x"]).then_inc(x_in, 16)
            act.dma_start(lng[:], io["ln_g"]).then_inc(consts_in, 16)
            act.dma_start(lnb[:], io["ln_b"]).then_inc(consts_in, 16)
            act.dma_start(sinks[:], io["sinks"]).then_inc(consts_in, 16)
            act.dma_start(mem_raw, io["mem"]).then_inc(mem_in, 16)
            act.wait_ge(x_in, 16)
            for k in range(KC):
                act.activation(x_hi[:, k, :], x[:, k, :], ACT.Copy).then_inc(x_hi0, 1)
            for s in range(SLOTS - 1):
                round_slab(s)

            def up(st):
                z = st.sem

                def gate(base, i, p, q):
                    round_slab(base + 3, i)
                    act.wait_ge(slab_done, base + 1 + SLOTS * i)
                    if st.part or q >= 2:
                        act.wait_ge(z["hidden"], st.h0 + p - 1)
                    act.activation(gated[q % 2], bank[2 * (q % 2)][:], ACT.Silu).then_inc(z["gated"], 1)
                    round_slab(base + 4, i)

                def hi(p, q):
                    act.wait_ge(z["hidden"], st.h0 + p + 1)
                    act.activation(h_hi[:, bass.ds(p, 1), :].rearrange("p a t -> p (a t)"), hidden[q % 2],
                                   ACT.Copy).then_inc(z["hhi"], 1)

                lead = 2 - st.nf % 2
                for p in range(lead):
                    gate(st.s0 + 2 * p, 0, p, p)
                    if p:
                        hi(p - 1, p - 1)
                with act.Fori(0, (st.nf - lead) // 2) as i:
                    for k in range(2):
                        q = lead + k
                        gate(st.s0 + 2 * q, i, q + 2 * i, q)
                        hi(q - 1 + 2 * i, q - 1)
                hi(st.nf - 1, st.nf - 1)

            def out(st):
                if st is final:
                    for k in range(3, KC):
                        round_slab(st.s0 + k)
                else:
                    with act.Fori(0, 2) as i:
                        for k in range(4):
                            round_slab(st.s0 + k + 3, i)
                if st.last:
                    norm(st)

            def norm(st):
                c0 = KC * st.ln
                fill = MEM_FILL[st.ln][2] if st.ln in MEM_FILL else 0
                f0 = st.s0 + st.n
                if fill:
                    round_slab(f0 + 3)
                for j in range(KC):
                    act.wait_ge(ln["dev"], c0 + j + 1)
                    if j >= 4:
                        act.wait_ge(ln["var"], c0 + j - 3)
                    act.activation(square[j % 4], x[:, j, :], ACT.Square).then_inc(ln["sq"], 1)
                act.wait_ge(ln["var"], c0 + KC)
                act.activation(std, bank[B_VAR][:], ACT.Sqrt, bias=eps[:, 0:1]).then_inc(ln["std"], 1)
                for j in range(KC):
                    if j % 2 == 0 and 4 + j // 2 < min(fill + 3, 8):
                        round_slab(f0 + 4 + j // 2)
                    act.wait_ge(ln["norm"], c0 + j + 1)
                    b = lnb[:, st.ln, j:j + 1]
                    if st is not final:
                        act.activation(x_hi[:, j, :], x[:, j, :], ACT.Identity, bias=b)
                    act.activation(x[:, j, :], x[:, j, :], ACT.Identity, bias=b).then_inc(ln["xf"], 1)

            def memory(st):
                for k in range(1, st.n):
                    if k >= 4 and k + 4 < st.n + 3:
                        round_slab(st.s0 + k + 4)
                    if k % 2 == 0:
                        continue
                    act.wait_ge(slab_done, st.s0 + k + 1)
                    src = bank[FILL_BANKS[k // 2]]
                    c = st.h0 + k - 1
                    if c < KC:
                        dst = memkT[:, c:c + 2, :].rearrange("p c m -> p (c m)")
                        src = src[:]
                    else:
                        dst = memv[:, :, (c - KC) * P:(c - KC + 2) * P].rearrange("p i (s d) -> p i s d", s=2)
                        src = src[:].rearrange("p (s i d) -> p i s d", s=2, i=MT)
                    act.activation(dst, src, ACT.Copy).then_inc(mem_evac, 1)

            def kv(st):
                z = st.sem
                nfeat = {"kv_swa": 2, "kv_nsa": 4}[st.kind]
                if st.kind == "kv_nsa":
                    act.wait_ge(x_ready[st.x], KC)
                    for half in range(2):
                        r = slice(64 * half, 64 * half + 64)
                        act.dma_start(cw1[r], io["cmp_w1"]).then_inc(cmp_in, 16)
                        act.dma_start(cw2[r], io["cmp_w2"]).then_inc(cmp_in, 16)
                        act.dma_start(cpos[r], io["cmp_pos"]).then_inc(cmp_in, 16)
                for n in range(nfeat):
                    round_slab(st.s0 + n + 3)
                    act.wait_ge(slab_done, st.s0 + n + 1)
                    act.activation(keysT[:, n, :], bank[n % 4][:], ACT.Copy).then_inc(z["aevac"], 1)
                for n in range(nfeat, st.n):
                    round_slab(st.s0 + n + 3)
                if st.kind == "kv_nsa":
                    act.wait_ge(slab_done, st.s0 + 7)
                    act.activation(gates[:], bank[2][:, 0:512].rearrange("p (i n) -> p i n", i=NT)[:, :, 0:48],
                                   ACT.Exp, scale=-1.0).then_inc(z["gexp"], 1)
                    for n in range(2):
                        act.wait_ge(z["c1"], n + 1)
                        act.activation(ch1[n], bank[4 + n][:, 0:NCMP], ACT.Gelu_apprx_tanh).then_inc(z["c1g"], 1)
                    act.wait_ge(z["c2"], 1)
                    act.activation(kcmpT, bank[6][:, 0:NCMP], ACT.Copy).then_inc(z["c2e"], 1)
                    act.wait_ge(z["c2"], 2)
                    for half in range(2):
                        act.activation(vcmp[:, 64 * half:64 * half + 64], bank[7 - 4 * half][0:NCMP, 0:64],
                                       ACT.Copy).then_inc(z["c2e"], 1)

            def attention(st):
                z = st.sem
                kind = st.kind[4:]
                T = attention_units(kind)
                nslab = 2 if kind == "x" else 1
                qs = qs_mem if kind == "x" else qs_mix
                slopes = slope_nsa if kind == "nsa" else slope_swa
                span = slice(0, 640) if kind == "nsa" else slice(640, 896)

                def q_evac(b, i):
                    for n in range(nslab):
                        c = nslab * b.b + n
                        round_slab(st.s0 + c + 3, i)
                        act.wait_ge(slab_done, st.s0 + c + 1 + SLOTS * i)
                        act.activation(qs[b.b % 2][:, n, :], bank[0][:], ACT.Copy,
                                       scale=1 / 16 if kind == "x" else 0.125).then_inc(z["q"], 1)

                def bias(h, i):
                    if h >= 2:
                        last = max(u.u for u in T.units if u.head == h - 2)
                        act.wait_ge(z["add"], last + 1 + T.n * i)
                    act.activation(biasb[h % 2][:, 0:span.stop - span.start], dist[:, span], ACT.Copy,
                                   scale=slopes[:, bass.ds(h + T.heads * i, 1)]).then_inc(z["bias"], 1)

                def softmax_exp(u, i):
                    act.wait_ge(z["nm"], u.u + 1 + T.n * i)
                    if u.u >= 3:
                        act.wait_ge(z["t"], u.u - 2 + T.n * i)
                        if T.units[u.u - 3].br == "cmp":
                            n = sum(v.br == "cmp" for v in T.units[:u.u - 2])
                            act.wait_ge(z["csum"], n + 4 * 2 * i)
                    if u.br == "cmp":
                        dst, src = (t[:, 0:P].rearrange("p (i n) -> p i n", i=NT)[:, :, 0:NCMP]
                                    for t in (prob[u.u % 3], sS[u.u % 2]))
                        act.activation(dst, src, ACT.Exp).then_inc(z["p"], 1)
                        return
                    w = P * len(u.keys)
                    slot = 4 * (u.g % 4) + (0 if kind == "x" else u.i)
                    ring = 16 * (u.g % 8 // 4)
                    src = bank[B_S + u.u % 2] if kind == "x" else sS[u.u % 2]
                    act.activation(prob[u.u % 3][:, 0:w], src[:, 0:w], ACT.Exp, bias=negm[:, slot:slot + 1],
                                   accum_out=sums[:, slot + ring:slot + ring + 1]).then_inc(z["p"], 1)

                def sink(g, i):
                    h = T.groups[g].head
                    act.activation(sinkexp[:, 4 * (g % 4):4 * (g % 4) + 4], negm[:, 4 * (g % 4):4 * (g % 4) + 4],
                                   ACT.Exp, bias=sinks[:, bass.ds(h + T.heads * i, 1)]).then_inc(z["sink"], 1)

                def probT_evac(u, i):
                    act.wait_ge(z["t"], u.u + 1 + T.n * i)
                    if u.u >= 2:
                        act.wait_ge(z["pv"], u.u - 1 + T.n * i)
                    if u.br == "cmp":
                        act.activation(probT[u.u % 2][0:NCMP, :], bank[B_T + u.u % 2][0:NCMP, :],
                                       ACT.Copy).then_inc(z["pt"], 1)
                    else:
                        w = P * len(u.keys)
                        act.activation(probT[u.u % 2][:, 0:w], bank[B_T + u.u % 2][:, 0:w], ACT.Copy).then_inc(z["pt"], 1)

                def out_hi(b, i):
                    for n in range(nslab):
                        c = nslab * b.b + n
                        act.wait_ge(z["ot"], c + 1 + SLOTS * i)
                        act.activation(h_hi[:, bass.ds(c + SLOTS * i, 1), :].rearrange("p a t -> p (a t)"),
                                       bank[B_OT][:], ACT.Copy).then_inc(z["ohi"], 1)

                if kind != "x":
                    act.wait_ge(dist_ready, 4)
                with act.Fori(0, SLOTS * 2 // (T.nb * nslab)) as i:
                    for t in range(T.n + 9):
                        for b in T.blocks:
                            if t == max(b.first - 1 - nslab, 0):
                                q_evac(b, i)
                        if kind != "x":
                            for h in range(T.heads):
                                first = min(u.u for u in T.units if u.head == h)
                                if t == max(first - 2, 0):
                                    bias(h, i)
                        if 2 <= t <= T.n + 1:
                            probT_evac(T.units[t - 2], i)
                        if t < T.n:
                            softmax_exp(T.units[t], i)
                            if kind == "swa" and T.units[t].last:
                                sink(T.units[t].g, i)
                        for b in T.blocks:
                            if t == b.last + 7:
                                out_hi(b, i)

            for st in stages:
                if st.kind == "up":
                    up(st)
                elif st.kind == "out":
                    out(st)
                elif st.kind == "mem":
                    memory(st)
                elif st.kind.startswith("kv"):
                    kv(st)
                else:
                    attention(st)
                if st.id == 0:
                    act.wait_ge(mem_in, 16)
                    act.activation(mem_hi, mem_raw, ACT.Copy).then_inc(mem_rounded, 1)

        @block.vector
        def _(dve):
            dve.wait_ge(iota_done, 3)
            dve.tensor_copy(dist[:, 0:512], dist_i[:, 0:512]).then_inc(dist_f, 1)
            dve.tensor_scalar(dist[:, 512:640], dist_i[:, 512:640], 15.5, None, ALU.add).then_inc(dist_f, 1)
            dve.tensor_copy(dist[:, 640:896], dist_i[:, 640:896]).then_inc(dist_f, 1)
            dve.wait_ge(consts_in, 48)
            dve.wait_ge(x_in, 16)
            for k in range(KC):
                dve.wait_ge(x_hi0, k + 1)
                dve.tensor_tensor(x_lo[:, k, :], x[:, k, :], x_hi[:, k, :].bitcast(F32),
                                  ALU.subtract).then_inc(x_ready[0], 1)

            def up(st):
                z = st.sem

                def hid(base, i, p, q):
                    dve.wait_ge(z["gated"], st.h0 + p + 1)
                    dve.wait_ge(slab_done, base + 2 + SLOTS * i)
                    if st.part or q >= 2:
                        dve.wait_ge(z["hhi"], st.h0 + p - 1)
                        dve.wait_ge(z["hlo"], st.h0 + p - 1)
                    dve.scalar_tensor_tensor(out=hidden[q % 2], in0=gated[q % 2], scalar=0.5,
                                             in1=bank[2 * (q % 2) + 1][:], op0=ALU.mult,
                                             op1=ALU.mult).then_inc(z["hidden"], 1)

                def lo(p, q):
                    dve.wait_ge(z["hhi"], st.h0 + p + 1)
                    dve.tensor_tensor(h_lo[:, bass.ds(p, 1), :].rearrange("p a t -> p (a t)"), hidden[q % 2],
                                      h_hi[:, bass.ds(p, 1), :].rearrange("p a t -> p (a t)").bitcast(F32),
                                      ALU.subtract).then_inc(z["hlo"], 1)

                lead = 2 - st.nf % 2
                for p in range(lead):
                    hid(st.s0 + 2 * p, 0, p, p)
                    if p:
                        lo(p - 1, p - 1)
                with dve.Fori(0, (st.nf - lead) // 2) as i:
                    for k in range(2):
                        q = lead + k
                        hid(st.s0 + 2 * q, i, q + 2 * i, q)
                        lo(q - 1 + 2 * i, q - 1)
                lo(st.nf - 1, st.nf - 1)

            def out(st):
                z = st.sem
                dve.sem_inc(z["free"], 2)
                if st.last:
                    dve.memset(ysum, 0.0).then_inc(ln["sum"], 1)
                with dve.Fori(0, 2) as i:
                    for k in range(4):
                        j = k + 4 * i
                        xj = x[:, bass.ds(j, 1), :].rearrange("p a t -> p (a t)")
                        dve.wait_ge(slab_done, st.s0 + k + 1 + SLOTS * i)
                        if st.first:
                            dve.scalar_tensor_tensor(out=xj, in0=xj, scalar=ALPHA, in1=bank[k % 2][:],
                                                     op0=ALU.mult, op1=ALU.add).then_inc(z["free"], 1)
                        else:
                            dve.tensor_tensor(xj, xj, bank[k % 2][:], ALU.add).then_inc(z["free"], 1)
                        if st.last:
                            dve.wait_ge(z["free"], (2 + KC) * st.part + 3 + j)
                            dve.wait_ge(ln["sum"], (KC + 1) * st.ln + 1 + j)
                            dve.tensor_tensor(ysum, ysum, xj, ALU.add).then_inc(ln["sum"], 1)
                if st.last:
                    norm(st)

            def norm(st):
                c0 = KC * st.ln
                dve.wait_ge(ln["mu"], st.ln + 1)
                for j in range(KC):
                    dve.tensor_tensor(x[:, j, :], x[:, j, :], bank[B_MU][:], ALU.subtract).then_inc(ln["dev"], 1)
                dve.wait_ge(ln["std"], st.ln + 1)
                dve.reciprocal(rstd, std).then_inc(ln["rstd"], 1)
                dve.wait_ge(ln["rstd"], st.ln + 1)
                dve.wait_ge(ln["sq"], c0 + KC)
                if st.ln == 0:
                    dve.wait_ge(consts_in, 48)

                def lo(j):
                    dve.wait_ge(ln["xf"], c0 + j + 1)
                    dve.tensor_tensor(x_lo[:, j, :], x[:, j, :], x_hi[:, j, :].bitcast(F32),
                                      ALU.subtract).then_inc(x_ready[st.ln + 1], 1)

                for j in range(KC):
                    dve.scalar_tensor_tensor(out=x[:, j, :], in0=x[:, j, :], scalar=lng[:, st.ln, j:j + 1],
                                             in1=rstd, op0=ALU.mult, op1=ALU.mult).then_inc(ln["norm"], 1)
                    if j >= 2 and st is not final:
                        lo(j - 2)
                if st is not final:
                    lo(KC - 2)
                    lo(KC - 1)

            def kv(st):
                z = st.sem
                if st.kind == "kv_swa":
                    for n in range(2):
                        dve.wait_ge(slab_done, st.s0 + 3 + n)
                        dve.tensor_copy(vals[:, n, :, :].rearrange("p i d -> p (i d)"),
                                        bank[2 + n][:]).then_inc(z["devac"], 1)
                else:
                    dve.wait_ge(cmp_in, 96)
                    for n in range(2):
                        dve.wait_ge(z["aevac"], 3 + n)
                        src = keysT[:, 2 + n, :]
                        toks = bass.AP(src.tensor, src.offset, [list(src.ap[0]), [1, CL], [16, NCMP]])
                        dve.tensor_tensor(cblk[n], toks, cpos[:, n, :, None].to_broadcast([P, CL, NCMP]),
                                          ALU.add).then_inc(z["blkk"], 1)
                    for n in range(2):
                        dve.wait_ge(slab_done, st.s0 + 5 + n)
                        dve.tensor_copy(vals[:, n, :, :].rearrange("p i d -> p (i d)"), bank[n][:]).then_inc(z["devac"], 1)
                    dve.wait_ge(z["gexp"], 1)
                    dve.tensor_scalar(gates[:], gates[:], 1.0, None, ALU.add).then_inc(z["gadd"], 1)
                    dve.wait_ge(z["gadd"], 1)
                    dve.reciprocal(gates[:], gates[:]).then_inc(z["gate"], 1)

            def attention(st):
                z = st.sem
                kind = st.kind[4:]
                T = attention_units(kind)
                nslab = 2 if kind == "x" else 1
                otok = otok_mem if kind == "x" else otok_mix
                links = [0]
                per_turn = {"swa": 2 * T.ng, "x": T.ng, "nsa": 0}[kind]
                if kind == "nsa":
                    per_turn = sum(6 if g.br == "cmp" else 3 for g in T.groups)

                def link(ins, i):
                    links[0] += 1
                    ins.then_inc(z["chain"], 1)
                    dve.wait_ge(z["chain"], links[0] + per_turn * i)

                def add(u, i):
                    dve.wait_ge(z["s"], u.u + 1 + T.n * i)
                    slot = 4 * (u.g % 4) + (0 if kind == "x" else u.i)
                    src = bank[B_S + u.u % 2]
                    if kind == "x":
                        if u.u >= 4:
                            dve.wait_ge(z["p"], u.u - 3 + T.n * i)
                        dve.reduce_max(rowmax[:, slot:slot + 1], src[:, 0:MEM], AX.X).then_inc(z["add"], 1)
                        dve.wait_ge(z["add"], u.u + 1 + T.n * i)
                        dve.tensor_scalar(negm[:, slot:slot + 1], rowmax[:, slot:slot + 1], -1.0, None,
                                          ALU.mult).then_inc(z["nm"], 1)
                        return
                    dve.wait_ge(z["bias"], u.head + 1 + T.heads * i)
                    if u.u >= 2:
                        dve.wait_ge(z["p"], u.u - 1 + T.n * i)
                    bias = biasb[u.head % 2]
                    if u.br == "cmp":
                        def blocks(t):
                            return t.rearrange("p (i n) -> p i n", i=NT)[:, :, 0:NCMP]

                        s3 = blocks(sS[u.u % 2][:, 0:P])
                        m = cmpmax
                        link(dve.tensor_tensor(s3, blocks(src[:, 0:P]), blocks(bias[:, 512:640]), ALU.add), i)
                        link(dve.tensor_reduce(m, s3, AX.X, ALU.max), i)
                        link(dve.tensor_scalar(m, m, -1.0e29, None, ALU.max), i)
                        dve.tensor_tensor(s3, s3, m[:, :, None].to_broadcast([P, NT, NCMP]),
                                          ALU.subtract).then_inc(z["nm"], 1)
                        dve.sem_inc(z["add"], 1)
                        return
                    w = P * len(u.keys)
                    b0 = (SEQ if kind == "nsa" else 256) - w
                    dve.sem_inc(cleared, 1)
                    dve.tensor_tensor_reduce(sS[u.u % 2][:, 0:w], src[:, 0:w], bias[:, b0:b0 + w], 1.0, -3.0e38,
                                             ALU.add, ALU.max, rowmax[:, slot:slot + 1]).then_inc(z["add"], 1)
                    dve.wait_ge(z["add"], u.u + 1 + T.n * i)
                    if kind == "swa":
                        dve.tensor_scalar(negm[:, slot:slot + 1], rowmax[:, slot:slot + 1],
                                          sinks[:, bass.ds(u.head + T.heads * i, 1)], -1.0,
                                          ALU.max, ALU.mult).then_inc(z["nm"], 1)
                    else:
                        dve.tensor_scalar(negm[:, slot:slot + 1], rowmax[:, slot:slot + 1], -1.0, None,
                                          ALU.mult).then_inc(z["nm"], 1)

                def cmp_sum(u, i):
                    dve.wait_ge(z["p"], u.u + 1 + T.n * i)
                    slot = 4 * (u.g % 8)
                    p3 = prob[u.u % 3][:, 0:P].rearrange("p (i n) -> p i n", i=NT)
                    dve.tensor_reduce(sums[:, slot:slot + 4], p3[:, :, 0:NCMP], AX.X, ALU.add).then_inc(z["csum"], 1)

                def finish(g, i):
                    slot = 4 * (g.g % 8)
                    src = bank[B_PV + g.g % 2]
                    dve.wait_ge(z["p"], g.last + 1 + T.n * i)
                    if kind == "x":
                        u = T.units[g.first]
                        r = rinv[:, g.g % 2:g.g % 2 + 1]
                        if g.g >= 2:
                            dve.wait_ge(z["fin"], g.g - 1 + T.ng * i)
                        link(dve.reciprocal(r, sums[:, slot:slot + 1]), i)
                        dve.wait_ge(z["pv"], u.u + 1 + T.n * i)
                        if u.first and g.b >= 2:
                            dve.wait_ge(z["ot"], 2 * (g.b - 1) + SLOTS * i)
                        dst = otok[g.b % 2].rearrange("p (i d) -> p i d", i=NT)[:, u.i, :]
                        dve.tensor_scalar(dst, src[:, 0:256], r, None, ALU.mult).then_inc(z["fin"], 1)
                        return
                    dst = otok[g.b % 2][:, 0:512].rearrange("p (i h d) -> p i h d", i=NT, h=2)[:, :, g.half, :]
                    s3 = src[:, 0:256].rearrange("p (i d) -> p i d", i=NT)
                    if kind == "swa":
                        dve.wait_ge(z["sink"], g.g + 1 + T.ng * i)
                        link(dve.tensor_tensor(tot, sums[:, slot:slot + 4], sinkexp[:, 4 * (g.g % 4):4 * (g.g % 4) + 4], ALU.add), i)
                        link(dve.reciprocal(rinv, tot), i)
                        r = rinv
                    else:
                        br = ("cmp", "sel", "win").index(g.br)
                        if br == 0:
                            n = sum(v.br == "cmp" for v in T.groups[:g.g + 1])
                            dve.wait_ge(z["csum"], n + 8 * i)
                            link(dve.tensor_scalar(tot, sums[:, slot:slot + 4], 1.0e-30, None, ALU.max), i)
                            link(dve.reciprocal(rinv, tot), i)
                        else:
                            link(dve.reciprocal(rinv, sums[:, slot:slot + 4]), i)
                        col = bass.ds(16 * br + g.head + T.heads * i, 1)
                        gt = gates[:, :, col].rearrange("p i a -> p (i a)")
                        link(dve.tensor_tensor(rgate, rinv, gt, ALU.mult), i)
                        r = rgate
                    dve.wait_ge(z["pv"], g.last + 1 + T.n * i)
                    if g.b >= 2 and g.first == T.blocks[g.b].first:
                        dve.wait_ge(z["ot"], g.b - 1 + SLOTS * i)
                    rb = r[:, :, None].to_broadcast([P, NT, 64])
                    if g.br in ("swa", "cmp"):
                        dve.tensor_tensor(dst, s3, rb, ALU.mult).then_inc(z["fin"], 1)
                    else:
                        t3 = otmp.rearrange("p (i d) -> p i d", i=NT)
                        link(dve.tensor_tensor(t3, s3, rb, ALU.mult), i)
                        dve.wait_ge(z["fin"], g.g + T.ng * i)
                        dve.tensor_tensor(dst, dst, t3, ALU.add).then_inc(z["fin"], 1)

                def out_lo(b, i):
                    for n in range(nslab):
                        c = nslab * b.b + n
                        dve.wait_ge(z["ohi"], c + 1 + SLOTS * i)
                        at = bass.ds(c + SLOTS * i, 1)
                        dve.tensor_tensor(h_lo[:, at, :].rearrange("p a t -> p (a t)"), bank[B_OT][:],
                                          h_hi[:, at, :].rearrange("p a t -> p (a t)").bitcast(F32),
                                          ALU.subtract).then_inc(z["olo"], 1)

                with dve.Fori(0, SLOTS * 2 // (T.nb * nslab)) as i:
                    for t in range(T.n + 9):
                        if t < T.n:
                            add(T.units[t], i)
                        if 1 <= t <= T.n and T.units[t - 1].br == "cmp":
                            cmp_sum(T.units[t - 1], i)
                        for g in T.groups:
                            if t == g.last + 4:
                                finish(g, i)
                        for b in T.blocks:
                            if t == b.last + 7:
                                out_lo(b, i)
                    assert links[0] == per_turn, (links, per_turn)

            for st in stages:
                if st.kind == "up":
                    up(st)
                elif st.kind == "out":
                    out(st)
                elif st.kind == "mem":
                    continue
                elif st.kind.startswith("kv"):
                    kv(st)
                else:
                    attention(st)
                if st.id == 0:
                    dve.wait_ge(mem_rounded, 1)
                    dve.tensor_tensor(mem_lo, mem_raw, mem_hi.bitcast(F32), ALU.subtract).then_inc(mem_split, 1)

        @block.tensor
        def _(pe):
            def slab_ready(base, i):
                pe.wait_ge(hi_ready, base + 1 + SLOTS * i)
                pe.wait_ge(lo_ready, base + 1 + SLOTS * i)

            def product(base, dst, m_hi, m_lo, n, chunk_wait=None):
                slot = base % SLOTS
                for k in range(n):
                    if chunk_wait is not None:
                        pe.wait_ge(chunk_wait[0], chunk_wait[1] + k + 1)
                    w = slice(k * P, (k + 1) * P)
                    pe.matmul(dst, w_hi[slot][:, w], m_hi[:, k, :], start=k == 0, stop=False)
                    pe.matmul(dst, w_hi[slot][:, w], m_lo[:, k, :], start=False, stop=False)
                    last = pe.matmul(dst, w_lo[slot][:, w], m_hi[:, k, :], start=False, stop=k == n - 1)
                last.then_inc(slab_done, 1)

            def product_tok(base, dst, s_hi, s_lo, tiles):
                slot = base % SLOTS
                for i in range(tiles):
                    tok = slice(i * P, (i + 1) * P)
                    for k in range(KC):
                        w = slice(k * P, (k + 1) * P)
                        o = dst[:, i * P:(i + 1) * P]
                        pe.matmul(o, s_hi[:, k, tok], w_hi[slot][:, w], start=k == 0, stop=False)
                        pe.matmul(o, s_hi[:, k, tok], w_lo[slot][:, w], start=False, stop=False)
                        last = pe.matmul(o, s_lo[:, k, tok], w_hi[slot][:, w], start=False, stop=k == KC - 1)
                last.then_inc(slab_done, 1)

            def up(st):
                z = st.sem

                def pair(base, i, p, q):
                    if q == 1 and fill_banks(st):
                        pe.wait_ge(mem_evac, fill_banks(st))
                    for n, used in enumerate((z["gated"], z["hidden"])):
                        slab_ready(base + n, i)
                        if st.part or q >= 2:
                            pe.wait_ge(used, st.h0 + p - 1)
                        product(base + n, bank[2 * (q % 2) + n][:], x_hi, x_lo, KC,
                                (x_ready[st.x], 0) if q == 0 and n == 0 and st.part == 0 else None)

                if st.part:
                    pe.wait_ge(prior(st).sem["free"], (2 + KC) * st.part)
                lead = 2 - st.nf % 2
                for p in range(lead):
                    pair(st.s0 + 2 * p, 0, p, p)
                with pe.Fori(0, (st.nf - lead) // 2) as i:
                    for k in range(2):
                        pair(st.s0 + 2 * (lead + k), i, lead + k + 2 * i, lead + k)

            def out(st):
                z = st.sem
                if st.of != "ffn":
                    pe.wait_ge(prior(st).sem["olo"], KC)
                with pe.Fori(0, 2) as i:
                    for k in range(4):
                        slab_ready(st.s0 + k, i)
                        pe.wait_ge(z["free"], (2 + KC) * st.part + k + 1 + 4 * i)
                        product(st.s0 + k, bank[k % 2][:], h_hi, h_lo, st.nf,
                                (prior(st).sem["hlo"], st.h0) if st.of == "ffn" and k == 0 else None)
                if st.last:
                    pe.wait_ge(pool_set, 3 + 2 * HEADS + 1)
                    pe.wait_ge(ln["sum"], (KC + 1) * (st.ln + 1))
                    pe.matmul(bank[B_MU][:], ones[:], ysum, start=True, stop=True).then_inc(ln["mu"], 1)
                    for j in range(KC):
                        pe.wait_ge(ln["sq"], KC * st.ln + j + 1)
                        pe.matmul(bank[B_VAR][:], ones[:], square[j % 4], start=j == 0,
                                  stop=j == KC - 1).then_inc(ln["var"], 1)

            def memory(st):
                if st.ln == 0:
                    pe.wait_ge(mem_split, 1)
                for n in range(st.n):
                    slab_ready(st.s0 + n, 0)
                    dst = bank[FILL_BANKS[n // 2]][:, MEM * (n % 2):MEM * (n % 2 + 1)]
                    if st.h0 < KC:
                        product(st.s0 + n, dst, mem_hi, mem_lo, KC)
                    else:
                        product_tok(st.s0 + n, dst, mem_hi, mem_lo, MT)

            def kv(st):
                z = st.sem
                nfeat = 2 if st.kind == "kv_swa" else 4
                for n in range(st.n):
                    slab_ready(st.s0 + n, 0)
                    if n >= 4:
                        pe.wait_ge(z["aevac"], n - 3)
                    if n == 2:
                        pe.wait_ge(mem_evac, fill_banks(st))
                    if n < nfeat:
                        product(st.s0 + n, bank[n % 4][:], x_hi, x_lo, KC, (x_ready[st.x], 0) if n == 0 else None)
                    else:
                        product_tok(st.s0 + n, bank[n % 4], x_hi, x_lo, NT)
                if st.kind == "kv_nsa":
                    for n in range(2):
                        pe.wait_ge(z["blkk"], n + 1)
                        for half in range(2):
                            r = slice(64 * half, 64 * half + 64)
                            for l in range(CL):
                                last = pe.matmul(bank[4 + n][r, 0:NCMP], cw1[r, n, l, :], cblk[n][r, l, :],
                                                 start=l == 0, stop=l == CL - 1)
                        last.then_inc(z["c1"], 1)
                    pe.wait_ge(z["c1g"], 1)
                    for half in range(2):
                        r = slice(64 * half, 64 * half + 64)
                        last = pe.matmul(bank[6][r, 0:NCMP], cw2[r, 0, :], ch1[0][r, :], start=True, stop=True)
                    last.then_inc(z["c2"], 1)
                    pe.wait_ge(z["c1g"], 2)
                    for half in range(2):
                        r = slice(64 * half, 64 * half + 64)
                        last = pe.matmul(bank[7 - 4 * half][0:NCMP, 0:64], ch1[1][r, :], cw2[r, 1, :],
                                         start=True, stop=True)
                    last.then_inc(z["c2"], 1)

            def attention(st):
                z = st.sem
                kind = st.kind[4:]
                T = attention_units(kind)
                nslab = 2 if kind == "x" else 1
                qs, otok = (qs_mem, otok_mem) if kind == "x" else (qs_mix, otok_mix)

                def q_block(b, i):
                    for n in range(nslab):
                        c = nslab * b.b + n
                        slab_ready(st.s0 + c, i)
                        if c:
                            pe.wait_ge(z["q"], c + SLOTS * i)
                        product(st.s0 + c, bank[0][:], x_hi, x_lo, KC,
                                (x_ready[st.x], 0) if kind == "x" and c == 0 else None)

                def scores(u, i):
                    if kind == "x" and u.u == 0:
                        pe.wait_ge(mem_evac, fill_banks(st))
                    if u.u == T.blocks[u.b].first:
                        pe.wait_ge(z["q"], nslab * (u.b + 1) + SLOTS * i)
                    if u.u >= 2:
                        pe.wait_ge(z["p"] if kind == "x" else z["add"], u.u - 1 + T.n * i)
                    dst = bank[B_S + u.u % 2]
                    q = qs[u.b % 2]
                    r = slice(64 * u.half, 64 * u.half + 64)
                    if u.br == "cmp":
                        for n in range(NT):
                            last = pe.matmul(dst[:, 32 * n:32 * n + NCMP], q[r, 0, n * P:(n + 1) * P],
                                             kcmpT[r, :], start=True, stop=True)
                    elif kind == "x":
                        for n in range(2):
                            last = pe.matmul(dst[:, 0:MEM], q[:, n, u.i * P:(u.i + 1) * P],
                                             memkT[:, bass.ds(2 * u.b + n + 4 * i, 1), :].rearrange("p a m -> p (a m)"),
                                             start=n == 0, stop=n == 1)
                    else:
                        kt = {"sel": 0, "win": 1, "swa": u.b % 2}[u.br]
                        last = pe.matmul(dst[:, 0:P * len(u.keys)], q[r, 0, u.i * P:(u.i + 1) * P],
                                         keysT[r, kt, u.keys[0] * P:(u.keys[-1] + 1) * P], start=True, stop=True)
                    last.then_inc(z["s"], 1)

                def transposes(u, i):
                    pe.wait_ge(z["p"], u.u + 1 + T.n * i)
                    if u.u >= 2:
                        pe.wait_ge(z["pt"], u.u - 1 + T.n * i)
                    dst, src = bank[B_T + u.u % 2], prob[u.u % 3]
                    if u.br == "cmp":
                        for n in range(NT):
                            last = pe.transpose(dst[0:NCMP, n * P:(n + 1) * P], src[:, 32 * n:32 * n + NCMP], ident[:])
                    else:
                        for n in range(len(u.keys)):
                            last = pe.transpose(dst[:, n * P:(n + 1) * P], src[:, n * P:(n + 1) * P], ident[:])
                    last.then_inc(z["t"], 1)

                def values(u, i):
                    pe.wait_ge(z["pt"], u.u + 1 + T.n * i)
                    if u.first or kind == "x":
                        if u.g >= 2:
                            pe.wait_ge(z["fin"], u.g - 1 + T.ng * i)
                    dst, src = bank[B_PV + u.g % 2], probT[u.u % 2]
                    c = slice(64 * u.half, 64 * u.half + 64)
                    if u.br == "cmp":
                        for n in range(NT):
                            last = pe.matmul(dst[:, 64 * n:64 * n + 64], src[0:NCMP, n * P:(n + 1) * P], vcmp[:, c],
                                             start=True, stop=True)
                    elif kind == "x":
                        for n in range(MT):
                            last = pe.matmul(dst[:, 0:256], src[:, n * P:(n + 1) * P],
                                             memv[:, n, bass.ds(256 * u.b + 512 * i, 256)], start=n == 0, stop=n == MT - 1)
                    else:
                        v = {"sel": 0, "win": 1, "swa": u.b % 2}[u.br]
                        for n, key in enumerate(u.keys):
                            last = pe.matmul(dst[:, 64 * u.i:64 * u.i + 64], src[:, n * P:(n + 1) * P],
                                             vals[:, v, key, c], start=n == 0, stop=n == len(u.keys) - 1)
                    last.then_inc(z["pv"], 1)

                def out_transpose(b, i):
                    pe.wait_ge(z["fin"], b.groups + T.ng * i)
                    for n in range(nslab):
                        c = nslab * b.b + n
                        if c:
                            pe.wait_ge(z["olo"], c + SLOTS * i)
                        for k in range(NT):
                            width = 256 if kind == "x" else P
                            last = pe.transpose(bank[B_OT][:, k * P:(k + 1) * P],
                                                otok[b.b % 2][:, width * k + n * P:width * k + (n + 1) * P], ident[:])
                        last.then_inc(z["ot"], 1)

                before = prior(st)
                if kind != "x":
                    pe.wait_ge(before.sem["aevac"], {"swa": 2, "nsa": 4}[kind])
                    pe.wait_ge(before.sem["devac"], 2)
                if kind == "nsa":
                    pe.wait_ge(before.sem["c2e"], 3)
                    pe.wait_ge(before.sem["gate"], 1)
                with pe.Fori(0, SLOTS * 2 // (T.nb * nslab)) as i:
                    for t in range(T.n + 9):
                        for b in T.blocks:
                            if t == max(b.first - 3, 0):
                                q_block(b, i)
                        if t < T.n:
                            scores(T.units[t], i)
                        if 2 <= t <= T.n + 1:
                            transposes(T.units[t - 2], i)
                        if 3 <= t <= T.n + 2:
                            values(T.units[t - 3], i)
                        for b in T.blocks:
                            if t == b.last + 6:
                                out_transpose(b, i)

            for st in stages:
                if st.kind == "up":
                    up(st)
                elif st.kind == "out":
                    out(st)
                elif st.kind == "mem":
                    memory(st)
                elif st.kind.startswith("kv"):
                    kv(st)
                else:
                    attention(st)


def slabs(w):
    k, n = w.shape
    return w.reshape(k // P, P, n // P, P).transpose(2, 1, 0, 3).reshape(n // P, P, k)


def lay_out(a):
    w8, w7 = [], []
    mem_slabs = [slabs(w) for w in a["xattn_w_kv"]]

    def memory(ln):
        if ln in MEM_FILL:
            layer, c0, n = MEM_FILL[ln]
            w8.append(mem_slabs[layer][c0:c0 + n])

    def ffn(i, gate, up, down):
        g, u = slabs(a[gate][i]), slabs(a[up][i])
        at = 0
        for nf in FPARTS:
            w8.append(np.stack([g[at:at + nf], u[at:at + nf]], 1).reshape(2 * nf, P, D))
            d = slabs(a[down][i][at * P:(at + nf) * P])
            (w8 if nf == 8 else w7).append(d)
            at += nf

    for i in range(DEPTH):
        ffn(i, "ffn1_w_gate", "ffn1_w_up", "ffn1_w_down")
        memory(4 * i)
        kind = "swa" if i == 0 else "nsa"
        w_in, w_out = a[kind + "_w_in"][0], a[kind + "_w_out"][0]
        heads = [h for pair in head_pairs(kind) for h in pair]
        cols = [w_in[:, 64 * h:64 * h + 64] for h in heads]
        rest = w_in[:, D:]
        if kind == "swa":
            w8.append(slabs(rest))
        else:
            kc, vc, ks, vs, kw, vw = (rest[:, P * n:P * n + P] for n in range(6))
            gl = rest[:, 6 * P:].reshape(D, 3, HEADS)[:, :, heads].reshape(D, 48)
            gl = np.concatenate([gl, np.zeros((D, P - 48), gl.dtype)], 1)
            w8.append(slabs(np.concatenate([ks, kw, kc, vc, vs, vw, gl], 1)))
        w8.append(slabs(np.concatenate(cols, 1)))
        w8.append(slabs(np.concatenate([w_out[64 * h:64 * h + 64] for h in heads], 0)))
        memory(4 * i + 1)
        w8.append(slabs(a["xattn_w_q"][i]))
        w8.append(slabs(a["xattn_w_o"][i]))
        memory(4 * i + 2)
        ffn(i, "ffn2_w_gate", "ffn2_w_up", "ffn2_w_down")
        memory(4 * i + 3)

    def feature_major(t, n):
        return np.ascontiguousarray(t.reshape(n, KC, P).transpose(2, 1, 0))

    swa_heads = [h for pair in head_pairs("swa") for h in pair]
    return {
        "w8": np.concatenate(w8, 0),
        "w7": np.concatenate(w7, 0),
        "x": feature_major(a["x"][0], SEQ),
        "mem": feature_major(a["mem"][0], MEM),
        "ln_g": feature_major(a["ln_g"].reshape(NLN, D), NLN).transpose(0, 2, 1),
        "ln_b": feature_major(a["ln_b"].reshape(NLN, D), NLN).transpose(0, 2, 1),
        "sinks": np.broadcast_to(a["swa_sinks"][0][swa_heads], (P, HEADS)),
        "cmp_pos": a["nsa_cmp_pos"][0].transpose(2, 0, 1),
        "cmp_w1": a["nsa_cmp_w1"][0].transpose(2, 0, 1, 3),
        "cmp_w2": a["nsa_cmp_w2"][0].transpose(1, 0, 2),
    }


def kernel(**inputs):
    import concourse.bacc as bacc
    from concourse.bass_utils import run_bass_kernel_spmd

    arrays = {k: np.ascontiguousarray(v) for k, v in lay_out({k: np.asarray(v) for k, v in inputs.items()}).items()}
    nc = bacc.Bacc("TRN2", target_bir_lowering=False, num_devices=1)
    io = {k: nc.dram_tensor(k + "_dram", v.shape, mybir.dt.from_np(v.dtype), kind="ExternalInput").ap()
          for k, v in arrays.items()}
    io["out"] = nc.dram_tensor("out_dram", (P, KC, SEQ), F32, kind="ExternalOutput").ap()
    build(nc, io)
    r = run_bass_kernel_spmd(nc, [{k + "_dram": v for k, v in arrays.items()}], core_ids=[0])
    return r.results[0]["out_dram"].transpose(2, 1, 0).reshape(1, SEQ, D)
```

```python
from contextlib import ExitStack

import numpy as np
import concourse.bass as bass
from concourse import mybir

ALU = mybir.AluOpType
ACT = mybir.ActivationFunctionType
AX = mybir.AxisListType
F32 = mybir.dt.float32
F32R = mybir.dt.float32r
I32 = mybir.dt.int32

P = 128
D = 1024
KC = D // P
SEQ = 512
NT = SEQ // P
MEM = 256
MT = MEM // P
DEPTH = 2
HEADS = 16
FFN = 2816
FPARTS = (8, 7, 7)
NCMP = SEQ // 16 - 1
CL = 32
EPS = 1e-5
ALPHA = (2 * DEPTH) ** 0.25
MASKED = -1.0e34
SLOTS = 4
SLAB = KC * P
NLN = 4 * DEPTH
MEM_FILL = {0: (0, 0, 8), 1: (0, 8, 8), 2: (1, 0, 4), 3: (1, 4, 4), 4: (1, 8, 4), 5: (1, 12, 4)}
FILL_BANKS = (2, 3, 6, 7)

assert sum(FPARTS) * P == FFN


class Stage:

    def __init__(self, kind, s0, n, x=None, part=None, nf=None, h0=None, w=None, ln=None, first=None, last=None,
                 of=None):
        self.kind, self.s0, self.n, self.x, self.part, self.nf, self.h0 = kind, s0, n, x, part, nf, h0
        self.w, self.ln, self.first, self.last, self.of = w, ln, first, last, of
        self.id = self.sem = None


class Unit:

    def __init__(self, u, b, half, head, br, i, keys, g, first, last):
        self.u, self.b, self.half, self.head, self.br = u, b, half, head, br
        self.i, self.keys, self.g, self.first, self.last = i, keys, g, first, last


class Group:

    def __init__(self, g, br, b, half, head, first):
        self.g, self.br, self.b, self.half, self.head, self.first = g, br, b, half, head, first
        self.last = first


class Block:

    def __init__(self, b, first):
        self.b, self.first, self.last, self.groups = b, first, first, 0


class Turn:

    def __init__(self, kind):
        self.kind, self.units, self.groups, self.blocks = kind, [], [], []
        self.heads = self.n = self.ng = self.nb = 0


def kv_slabs(kind):
    if kind == "swa":
        return [("v", 0), ("v", 1), ("k", 0), ("k", 1)]
    return [("k", 2), ("k", 3), ("v", 0), ("v", 1), ("g", 2), ("k", 0), ("k", 1)]


def head_pairs(kind):
    if kind == "swa":
        return [(i, i + 4) if e == 0 else (8 + i, 12 + i) for i in range(4) for e in range(2)]
    return [(c, c + 8) for c in range(8)]


def plan():
    stages, chunks = [], []

    def stage(kind, sizes, **more):
        stages.append(Stage(kind, len(chunks), len(sizes), **more))
        chunks.extend(sizes)

    def memory(ln):
        if ln in MEM_FILL:
            layer, c0, n = MEM_FILL[ln]
            stage("mem", [KC] * n, h0=c0, w=(layer, 0), ln=ln)

    ln = 0

    def ffn(layer, which, ln):
        for part, nf in enumerate(FPARTS):
            h0 = sum(FPARTS[:part])
            stage("up", [KC] * (2 * nf), x=ln, part=part, nf=nf, h0=h0, w=(layer, which))
            stage("out", [nf] * KC, part=part, nf=nf, h0=h0, ln=ln, w=(layer, which),
                  first=part == 0, last=part == len(FPARTS) - 1, of="ffn")
        memory(ln)

    for layer in range(DEPTH):
        ffn(layer, 1, ln)
        ln += 1
        kind = "swa" if layer == 0 else "nsa"
        stage("kv_" + kind, [KC] * len(kv_slabs(kind)), x=ln)
        stage("att_" + kind, [KC] * KC, x=ln)
        stage("out", [KC] * KC, part=0, nf=KC, ln=ln, first=True, last=True, of=kind, w=(layer, 0))
        memory(ln)
        ln += 1
        stage("att_x", [KC] * KC, x=ln, w=(layer, 0))
        stage("out", [KC] * KC, part=0, nf=KC, ln=ln, first=True, last=True, of="x", w=(layer, 0))
        memory(ln)
        ln += 1
        ffn(layer, 2, ln)
        ln += 1
    return stages, chunks


def attention_units(kind):
    T = Turn(kind)
    nblocks = 4
    for b in range(nblocks):
        block = Block(b, len(T.units))
        for half in ((0,) if kind == "x" else (0, 1)):
            head = b if kind == "x" else 2 * b + half
            for br in (("cmp", "sel", "win") if kind == "nsa" else (kind,)):
                if br == "cmp":
                    tiles = [(0, None)]
                elif br in ("sel", "win"):
                    tiles = [(i, list(range(i + 1))) for i in range(NT)]
                elif br == "swa":
                    tiles = [(i, [k for k in (i - 1, i) if k >= 0]) for i in range(NT)]
                else:
                    tiles = [(i, list(range(MT))) for i in range(NT)]
                for n, (i, keys) in enumerate(tiles):
                    if n == 0 or kind == "x":
                        T.groups.append(Group(g=len(T.groups), br=br, b=b, half=half, head=head,
                                                        first=len(T.units)))
                    g = T.groups[-1]
                    g.last = len(T.units)
                    T.units.append(Unit(u=len(T.units), b=b, half=half, head=head, br=br, i=i,
                                                   keys=keys, g=g.g, first=n == 0, last=n == len(tiles) - 1))
        block.last = len(T.units) - 1
        block.groups = len(T.groups)
        T.blocks.append(block)
    T.heads = nblocks if kind == "x" else 2 * nblocks
    T.n, T.ng, T.nb = len(T.units), len(T.groups), nblocks
    return T


def build(nc, io):
    stages, chunks = plan()
    total = len(chunks)

    with ExitStack() as ctx:
        def sb(name, shape, dt=F32):
            return ctx.enter_context(nc.sbuf_tensor(name, shape, dt))

        def sem(name):
            return ctx.enter_context(nc.semaphore(name))

        x = sb("x", [P, KC, SEQ])
        x_hi = sb("x_hi", [P, KC, SEQ], F32R)
        x_lo = sb("x_lo", [P, KC, SEQ], F32R)
        h_hi = sb("h_hi", [P, 12, SEQ], F32R)
        h_lo = sb("h_lo", [P, 12, SEQ], F32R)
        w_raw = [sb(f"w_raw{i}", [P, SLAB]) for i in range(SLOTS)]
        w_hi = [sb(f"w_hi{i}", [P, SLAB], F32R) for i in range(SLOTS)]
        w_lo = [sb(f"w_lo{i}", [P, SLAB], F32R) for i in range(SLOTS)]
        mem_hi = h_hi[:, 8:12, :].rearrange("p a b -> p (a b)").rearrange("p (k m) -> p k m", k=KC)
        mem_lo = h_lo[:, 8:12, :].rearrange("p a b -> p (a b)").rearrange("p (k m) -> p k m", k=KC)

        kvs = sb("kvs", [P, 3264])
        mem_kv = sb("mem_kv", [P, 2 * MT * D])
        keysT = kvs[:, 0:2048].rearrange("p (n t) -> p n t", n=4)
        vals = kvs[:, 2048:3072].rearrange("p (n i d) -> p n i d", n=2, i=NT)
        kcmpT = kvs[:, 3072:3072 + NCMP]
        vcmp = kvs[0:NCMP, 3136:3136 + P]
        memkT = mem_kv[:, 0:KC * MEM].rearrange("p (c m) -> p c m", c=KC)
        memv = mem_kv[:, KC * MEM:].rearrange("p (i d) -> p i d", i=MT)
        mem_raw = kvs[:, 0:2048].rearrange("p (k m) -> p k m", k=KC)

        wk = sb("wk", [P, 7168])
        gated = [wk[:, 512 * i:512 * (i + 1)] for i in range(2)]
        hidden = [wk[:, 1024 + 512 * i:1024 + 512 * (i + 1)] for i in range(2)]
        ysum = wk[:, 2048:2560]
        std = wk[:, 2560:3072]
        rstd = wk[:, 3072:3584]
        square = [wk[:, 3584 + 512 * i:3584 + 512 * (i + 1)] for i in range(4)]
        biasb = [wk[:, 640 * i:640 * (i + 1)] for i in range(2)]
        sS = [wk[:, 1280 + 512 * i:1280 + 512 * (i + 1)] for i in range(2)]
        prob = [wk[:, (2304, 2816, 6656)[i]:(2304, 2816, 6656)[i] + 512] for i in range(3)]
        probT = [wk[:, 3328 + 512 * i:3328 + 512 * (i + 1)] for i in range(2)]
        otmp = wk[:, 6400:6656]
        assert MEM_FILL[5] == (1, 12, 4)
        feat = [wk[:, 512 * i:512 * (i + 1)] for i in range(4)]
        feat_nsa = [memv[:, 0, 512:1024], memv[:, 1, 512:1024], wk[:, 6400:6912]]
        qs_mix = [wk[:, 4352 + 512 * i:4352 + 512 * (i + 1)].rearrange("p (c t) -> p c t", c=1) for i in range(2)]
        otok_mix = [wk[:, 5376 + 512 * i:5376 + 512 * (i + 1)] for i in range(2)]
        qs_mem = [kvs[:, 1024 * i:1024 * (i + 1)].rearrange("p (c t) -> p c t", c=2) for i in range(2)]
        otok_mem = [kvs[:, 2048:3072], wk[:, 4352:5376]]
        cw1 = wk[:, 0:4096].rearrange("p (n l e) -> p n l e", n=2, l=CL)
        cblk = [wk[:, 4096 + 992 * i:4096 + 992 * (i + 1)].rearrange("p (l n) -> p l n", l=CL) for i in range(2)]
        cpos = wk[:, 6144:6208].rearrange("p (n l) -> p n l", n=2)
        cw2 = wk[:, 6208:6336].rearrange("p (n e) -> p n e", n=2)
        ch1 = [wk[:, 6336 + 32 * i:6336 + 32 * i + NCMP] for i in range(2)]

        lng = sb("lng", [P, NLN, KC])
        lnb = sb("lnb", [P, NLN, KC])
        ones = sb("ones", [P, P])
        ident = sb("ident", [P, P])
        slope_swa = sb("slope_swa", [P, HEADS])
        slope_nsa = sb("slope_nsa", [P, HEADS])
        sinks = sb("sinks", [P, HEADS])
        dist_i = mem_kv[:, 0:896].bitcast(I32)
        dist = sb("dist", [P, 896])
        eps = sb("eps", [P, 1])
        gates = sb("gates", [P, NT, 48])
        small = sb("small", [P, 112])
        negm = small[:, 0:16]
        sinkexp = small[:, 32:48]
        tot = small[:, 48:52]
        rinv = small[:, 52:56]
        rgate = small[:, 56:60]
        rowmax = small[:, 60:76]
        cmpmax = small[:, 76:80]
        sums = small[:, 80:112]

        bank = [ctx.enter_context(nc.psum_tensor(f"bank{i}", [P, 512], F32)) for i in range(8)]
        B_OT, B_PV, B_S, B_T, B_MU, B_VAR = 1, 2, 4, 6, 4, 5
        B_OUT = 6

        raw_landed = [sem(f"raw_landed{i}") for i in range(SLOTS)]
        hi_ready = sem("hi_ready")
        lo_ready = sem("lo_ready")
        slab_done = sem("slab_done")
        x_ready = [sem(f"x_ready{n}") for n in range(NLN)]
        x_in = [sem(f"x_in{i}") for i in range(4)]
        cleared = sem("cleared")
        x_hi0 = sem("x_hi0")
        consts_in = sem("consts_in")
        pool_set = sem("pool_set")
        iota_done = sem("iota_done")
        dist_f = sem("dist_f")
        dist_ready = sem("dist_ready")
        mem_in = sem("mem_in")
        mem_rounded = sem("mem_rounded")
        mem_split = sem("mem_split")
        mem_k_evac = sem("mem_k_evac")
        mem_v_feat = sem("mem_v_feat")
        mem_v_tr = sem("mem_v_tr")
        mem_v_evac = sem("mem_v_evac")
        cmp_in = sem("cmp_in")
        out_done = sem("out_done")
        ln = {k: sem("ln_" + k) for k in ("sum", "mu", "dev", "sq", "var", "std", "rstd", "norm", "hi", "xf")}
        for n, st in enumerate(stages):
            st.id = n
            if st.kind in ("up", "out") and st.part:
                st.sem = stages[n - 2].sem
                continue
            if st.kind == "up":
                names = ("gated", "hidden", "hhi", "hlo")
            elif st.kind == "out":
                names = ("free",)
            elif st.kind.startswith("kv"):
                names = ("aevac", "tr", "devac", "gexp", "gadd", "gate", "blkk", "c1", "c1g", "c2", "c2e")
                if st.kind == "kv_swa":
                    names = names[:3]
            elif st.kind == "mem":
                names = ()
            else:
                names = ("q", "s", "add", "nm", "p", "t", "pt", "pv", "fin", "chain", "ot", "ohi", "olo")
                names += {"att_x": (), "att_swa": ("bias", "sink"), "att_nsa": ("bias", "csum")}[st.kind]
            st.sem = {k: sem(f"{k}_{n}") for k in names}
        final = stages[-1]

        def fill_banks(st, values):
            return sum(m.n // 2 for m in stages[:st.id] if m.kind == "mem" and (m.h0 >= KC) == values)

        def memory_out(pe, st):
            if fill_banks(st, False):
                pe.wait_ge(mem_k_evac, fill_banks(st, False))
            if fill_banks(st, True):
                pe.wait_ge(mem_v_evac, fill_banks(st, True))

        def prior(st, kind=None):
            return next(s for s in reversed(stages[:st.id]) if kind is None or s.kind == kind)

        block = ctx.enter_context(nc.Block())

        def raw_count(base, i):
            return 16 * (base // SLOTS + 1) + 16 * i

        @block.sync
        def _(sp):
            def load(base, i, src):
                if base >= SLOTS:
                    sp.wait_ge(lo_ready, base - SLOTS + 1 + SLOTS * i)
                slot = base % SLOTS
                sp.dma_start(w_raw[slot][:, 0:src.shape[-1]], src).then_inc(raw_landed[slot], 16)

            runs = []
            at = {7: 0, 8: 0}
            for s, n in enumerate(chunks):
                if s < SLOTS or s == SLOTS or runs[-1][2] != n:
                    runs.append([s, 0, n, at[n]])
                runs[-1][1] += 1
                at[n] += 1
            for s0, count, n, row in runs:
                w = io["w%d" % n]
                turns = count // SLOTS
                if turns > 1:
                    with sp.Fori(0, turns) as i:
                        for k in range(SLOTS):
                            load(s0 + k, i, w[bass.ds(row + k + SLOTS * i, 1), :, :].rearrange("a p n -> (a p) n"))
                else:
                    turns = 0
                for k in range(SLOTS * turns, count):
                    load(s0 + k, 0, w[row + k, :, :])
            for j in range(KC):
                sp.wait_ge(ln["xf"], KC * final.ln + j + 1)
                sp.dma_start(io["out"][:, j, :], x[:, j, :]).then_inc(out_done, 16)
            sp.wait_ge(out_done, 16 * KC)

        @block.gpsimd
        def _(pool):
            pool.memset(ident[:], 0.0).then_inc(pool_set, 1)
            pool.memset(ones[:], 1.0 / D).then_inc(pool_set, 1)
            pool.memset(eps[:], EPS).then_inc(pool_set, 1)
            for kind, table in (("swa", slope_swa), ("nsa", slope_nsa)):
                for c, pair in enumerate(head_pairs(kind)):
                    for half in range(2):
                        pool.memset(table[:, 2 * c + half:2 * c + half + 1],
                                    float(2.0 ** (-8.0 * (pair[half] + 1) / HEADS))).then_inc(pool_set, 1)
            pool.iota(dist_i[:, 0:512], [[1, 512]], base=-384, channel_multiplier=-1).then_inc(iota_done, 1)
            pool.iota(dist_i[:, 512:640].rearrange("p (i n) -> p i n", i=NT), [[-128, NT], [16, 32]], base=0,
                      channel_multiplier=-1).then_inc(iota_done, 1)
            pool.iota(dist_i[:, 640:896], [[1, 256]], base=-128, channel_multiplier=-1).then_inc(iota_done, 1)
            pool.wait_ge(pool_set, 3)
            pool.affine_select(out=ident[:], in_=ident[:], compare_op=ALU.not_equal, fill=1.0, base=0,
                               pattern=[[-1, P]], channel_multiplier=1).then_inc(pool_set, 1)
            pool.wait_ge(dist_f, 3)
            pool.affine_select(out=dist[:, 0:512], in_=dist[:, 0:512], compare_op=ALU.is_ge, fill=MASKED, base=384,
                               pattern=[[-1, 512]], channel_multiplier=1).then_inc(dist_ready, 1)
            cd = dist[:, 512:640].rearrange("p (i n) -> p i n", i=NT)
            pool.affine_select(out=cd, in_=cd, compare_op=ALU.is_ge, fill=MASKED, base=-31,
                               pattern=[[128, NT], [-16, 32]], channel_multiplier=1).then_inc(dist_ready, 1)
            pool.affine_select(out=dist[:, 640:896], in_=dist[:, 640:896], compare_op=ALU.is_ge, fill=MASKED,
                               base=128, pattern=[[-1, 256]], channel_multiplier=1).then_inc(dist_ready, 1)
            pool.wait_ge(dist_ready, 3)
            pool.affine_select(out=dist[:, 640:896], in_=dist[:, 640:896], compare_op=ALU.is_ge, fill=MASKED,
                               base=-1, pattern=[[1, 256]], channel_multiplier=-1).then_inc(dist_ready, 1)

            def split(base, i, n):
                slot = base % SLOTS
                pool.wait_ge(hi_ready, base + 1 + SLOTS * i)
                pool.tensor_tensor(w_lo[slot][:, 0:n * P], w_raw[slot][:, 0:n * P],
                                   w_hi[slot][:, 0:n * P].bitcast(F32), ALU.subtract).then_inc(lo_ready, 1)

            s = 0
            while s < total:
                n = chunks[s]
                count = next((e for e in range(s, total) if chunks[e] != n), total) - s
                turns = count // SLOTS
                if turns:
                    with pool.Fori(0, turns) as i:
                        for k in range(SLOTS):
                            split(s + k, i, n)
                for k in range(SLOTS * turns, count):
                    split(s + k, 0, n)
                s += count

        @block.scalar
        def _(act):
            def round_slab(base, i=0):
                if base >= total:
                    return
                slot = base % SLOTS
                act.wait_ge(raw_landed[slot], raw_count(base, i))
                if base >= SLOTS:
                    act.wait_ge(slab_done, base - SLOTS + 1 + SLOTS * i)
                act.activation(w_hi[slot][:], w_raw[slot][:], ACT.Copy).then_inc(hi_ready, 1)

            for n in range(4):
                act.dma_start(x[:, 2 * n:2 * n + 2, :], io["x"][:, 2 * n:2 * n + 2, :]).then_inc(x_in[n], 16)
            act.dma_start(lng[:], io["ln_g"]).then_inc(consts_in, 16)
            act.dma_start(lnb[:], io["ln_b"]).then_inc(consts_in, 16)
            act.dma_start(sinks[:], io["sinks"]).then_inc(consts_in, 16)
            act.dma_start(mem_raw, io["mem"]).then_inc(mem_in, 16)
            round_slab(0)
            for k in range(KC):
                act.wait_ge(x_in[k // 2], 16)
                act.activation(x_hi[:, k, :], x[:, k, :], ACT.Copy).then_inc(x_hi0, 1)
            for s in range(1, SLOTS - 1):
                round_slab(s)

            def up(st):
                z = st.sem

                def gate(base, i, p, q):
                    round_slab(base + 3, i)
                    act.wait_ge(slab_done, base + 1 + SLOTS * i)
                    if st.part or q >= 2:
                        act.wait_ge(z["hidden"], st.h0 + p - 1)
                    act.activation(gated[q % 2], bank[2 * (q % 2)][:], ACT.Silu).then_inc(z["gated"], 1)
                    round_slab(base + 4, i)

                def hi(p, q):
                    act.wait_ge(z["hidden"], st.h0 + p + 1)
                    act.activation(h_hi[:, bass.ds(p, 1), :].rearrange("p a t -> p (a t)"), hidden[q % 2],
                                   ACT.Copy).then_inc(z["hhi"], 1)

                lead = 2 - st.nf % 2
                for p in range(lead):
                    gate(st.s0 + 2 * p, 0, p, p)
                    if p:
                        hi(p - 1, p - 1)
                with act.Fori(0, (st.nf - lead) // 2) as i:
                    for k in range(2):
                        q = lead + k
                        gate(st.s0 + 2 * q, i, q + 2 * i, q)
                        hi(q - 1 + 2 * i, q - 1)
                hi(st.nf - 1, st.nf - 1)

            def out(st):
                if st is final:
                    for k in range(3, KC):
                        round_slab(st.s0 + k)
                else:
                    with act.Fori(0, 2) as i:
                        for k in range(4):
                            round_slab(st.s0 + k + 3, i)
                if st.last:
                    norm(st)

            def norm(st):
                c0 = KC * st.ln
                fill = MEM_FILL[st.ln][2] if st.ln in MEM_FILL else 0
                f0 = st.s0 + st.n
                ahead = 3
                if fill:
                    round_slab(f0 + 3)
                    ahead = 4
                if fill == KC:
                    round_slab(f0 + 4)
                    ahead = 5
                for j in range(KC):
                    act.wait_ge(ln["dev"], c0 + j + 1)
                    if j >= 4:
                        act.wait_ge(ln["var"], c0 + j - 3)
                    act.activation(square[j % 4], x[:, j, :], ACT.Square).then_inc(ln["sq"], 1)
                if fill == KC:
                    round_slab(f0 + 5)
                    ahead = 6
                act.wait_ge(ln["var"], c0 + KC)
                act.activation(std, bank[B_VAR][:], ACT.Sqrt, bias=eps[:, 0:1]).then_inc(ln["std"], 1)
                for j in range(KC):
                    if fill and j % 2 == 0 and ahead + j // 2 < fill + 3:
                        round_slab(f0 + ahead + j // 2)
                    act.wait_ge(ln["norm"], c0 + j + 1)
                    b = lnb[:, st.ln, j:j + 1]
                    if st is final:
                        act.activation(x[:, j, :], x[:, j, :], ACT.Identity, bias=b).then_inc(ln["xf"], 1)
                    else:
                        act.activation(x_hi[:, j, :], x[:, j, :], ACT.Identity, bias=b).then_inc(ln["hi"], 1)
                if st is not final and not fill:
                    residual(st.ln)

            def residual(n):
                for j in range(KC):
                    act.wait_ge(x_ready[n + 1], j + 1)
                    act.activation(x[:, j, :], x[:, j, :], ACT.Identity,
                                   bias=lnb[:, n, j:j + 1]).then_inc(ln["xf"], 1)

            def memory(st):
                for k in range(1, st.n):
                    if st.n == KC and k == 6:
                        round_slab(st.s0 + st.n + 2)
                    if k % 2 == 0:
                        continue
                    act.wait_ge(slab_done, st.s0 + k + 1)
                    c = st.h0 + k - 1
                    if c < KC:
                        act.activation(memkT[:, c:c + 2, :].rearrange("p c m -> p (c m)"), bank[FILL_BANKS[k // 2]][:],
                                       ACT.Copy).then_inc(mem_k_evac, 1)
                    else:
                        act.activation(feat[k // 2], bank[FILL_BANKS[k // 2]][:],
                                       ACT.Copy).then_inc(mem_v_feat, 1)
                residual(st.ln)

            def kv(st):
                z = st.sem
                if st.kind == "kv_nsa":
                    act.wait_ge(x_ready[st.x], KC)
                    act.wait_ge(mem_v_tr, fill_banks(st, True))
                    for half in range(2):
                        r = slice(64 * half, 64 * half + 64)
                        act.dma_start(cw1[r], io["cmp_w1"]).then_inc(cmp_in, 16)
                        act.dma_start(cw2[r], io["cmp_w2"]).then_inc(cmp_in, 16)
                        act.dma_start(cpos[r], io["cmp_pos"]).then_inc(cmp_in, 16)
                for n, (what, m) in enumerate(kv_slabs(st.kind[3:])):
                    round_slab(st.s0 + n + 3)
                    act.wait_ge(slab_done, st.s0 + n + 1)
                    dst = keysT[:, m, :] if what == "k" else (feat if st.kind == "kv_swa" else feat_nsa)[m]
                    act.activation(dst, bank[n % 4][:], ACT.Copy).then_inc(z["aevac"], 1)
                if st.kind == "kv_nsa":
                    act.wait_ge(z["tr"], 3)
                    act.activation(gates[:], bank[3][:, 0:512].rearrange("p (i n) -> p i n", i=NT)[:, :, 0:48],
                                   ACT.Exp, scale=-1.0).then_inc(z["gexp"], 1)
                    for n in range(2):
                        act.wait_ge(z["c1"], n + 1)
                        act.activation(ch1[n], bank[4 + n][:, 0:NCMP], ACT.Gelu_apprx_tanh).then_inc(z["c1g"], 1)
                    act.wait_ge(z["c2"], 1)
                    act.activation(kcmpT, bank[6][:, 0:NCMP], ACT.Copy).then_inc(z["c2e"], 1)
                    act.wait_ge(z["c2"], 2)
                    for half in range(2):
                        act.activation(vcmp[:, 64 * half:64 * half + 64], bank[7 - 4 * half][0:NCMP, 0:64],
                                       ACT.Copy).then_inc(z["c2e"], 1)

            def attention(st):
                z = st.sem
                kind = st.kind[4:]
                T = attention_units(kind)
                nslab = 2 if kind == "x" else 1
                qs = qs_mem if kind == "x" else qs_mix
                slopes = slope_nsa if kind == "nsa" else slope_swa
                span = slice(0, 640) if kind == "nsa" else slice(640, 896)

                def q_evac(b, i):
                    for n in range(nslab):
                        c = nslab * b.b + n
                        round_slab(st.s0 + c + 3, i)
                        act.wait_ge(slab_done, st.s0 + c + 1 + SLOTS * i)
                        act.activation(qs[b.b % 2][:, n, :], bank[0][:], ACT.Copy,
                                       scale=1 / 16 if kind == "x" else 0.125).then_inc(z["q"], 1)

                def bias(h, i):
                    if h >= 2:
                        last = max(u.u for u in T.units if u.head == h - 2)
                        act.wait_ge(z["add"], last + 1 + T.n * i)
                    act.activation(biasb[h % 2][:, 0:span.stop - span.start], dist[:, span], ACT.Copy,
                                   scale=slopes[:, bass.ds(h + T.heads * i, 1)]).then_inc(z["bias"], 1)

                def softmax_exp(u, i):
                    act.wait_ge(z["nm"], u.u + 1 + T.n * i)
                    if u.u >= 3:
                        act.wait_ge(z["t"], u.u - 2 + T.n * i)
                        if T.units[u.u - 3].br == "cmp":
                            n = sum(v.br == "cmp" for v in T.units[:u.u - 2])
                            act.wait_ge(z["csum"], n + 4 * 2 * i)
                    if u.br == "cmp":
                        dst, src = (t[:, 0:P].rearrange("p (i n) -> p i n", i=NT)[:, :, 0:NCMP]
                                    for t in (prob[u.u % 3], sS[u.u % 2]))
                        act.activation(dst, src, ACT.Exp).then_inc(z["p"], 1)
                        return
                    w = P * len(u.keys)
                    slot = 4 * (u.g % 4) + (0 if kind == "x" else u.i)
                    ring = 16 * (u.g % 8 // 4)
                    src = bank[B_S + u.u % 2] if kind == "x" else sS[u.u % 2]
                    act.activation(prob[u.u % 3][:, 0:w], src[:, 0:w], ACT.Exp, bias=negm[:, slot:slot + 1],
                                   accum_out=sums[:, slot + ring:slot + ring + 1]).then_inc(z["p"], 1)

                def sink(g, i):
                    h = T.groups[g].head
                    act.activation(sinkexp[:, 4 * (g % 4):4 * (g % 4) + 4], negm[:, 4 * (g % 4):4 * (g % 4) + 4],
                                   ACT.Exp, bias=sinks[:, bass.ds(h + T.heads * i, 1)]).then_inc(z["sink"], 1)

                def probT_evac(u, i):
                    act.wait_ge(z["t"], u.u + 1 + T.n * i)
                    if u.u >= 2:
                        act.wait_ge(z["pv"], u.u - 1 + T.n * i)
                    if u.br == "cmp":
                        act.activation(probT[u.u % 2][0:NCMP, :], bank[B_T + u.u % 2][0:NCMP, :],
                                       ACT.Copy).then_inc(z["pt"], 1)
                    else:
                        w = P * len(u.keys)
                        act.activation(probT[u.u % 2][:, 0:w], bank[B_T + u.u % 2][:, 0:w], ACT.Copy).then_inc(z["pt"], 1)

                def out_hi(b, n, i):
                    c = nslab * b.b + n
                    act.wait_ge(z["ot"], c + 1 + SLOTS * i)
                    act.activation(h_hi[:, bass.ds(c + SLOTS * i, 1), :].rearrange("p a t -> p (a t)"),
                                   bank[B_OT][:], ACT.Copy).then_inc(z["ohi"], 1)

                if kind != "x":
                    act.wait_ge(dist_ready, 4)
                with act.Fori(0, SLOTS * 2 // (T.nb * nslab)) as i:
                    for t in range(T.n + 9):
                        for b in T.blocks:
                            if t == max(b.first - 1 - nslab, 0):
                                q_evac(b, i)
                        if kind != "x":
                            for h in range(T.heads):
                                first = min(u.u for u in T.units if u.head == h)
                                if t == max(first - 2, 0):
                                    bias(h, i)
                        if 2 <= t <= T.n + 1:
                            probT_evac(T.units[t - 2], i)
                        if t < T.n:
                            softmax_exp(T.units[t], i)
                            if kind == "swa" and T.units[t].last:
                                sink(T.units[t].g, i)
                        for b in T.blocks:
                            for n in range(nslab):
                                if t == b.last + 7 + 2 * n:
                                    out_hi(b, n, i)

            for st in stages:
                if st.kind == "up":
                    up(st)
                elif st.kind == "out":
                    out(st)
                elif st.kind == "mem":
                    memory(st)
                elif st.kind.startswith("kv"):
                    kv(st)
                else:
                    attention(st)
                if st.id == 0:
                    act.wait_ge(mem_in, 16)
                    act.activation(mem_hi, mem_raw, ACT.Copy).then_inc(mem_rounded, 1)

        @block.vector
        def _(dve):
            dve.wait_ge(iota_done, 3)
            dve.tensor_copy(dist[:, 0:512], dist_i[:, 0:512]).then_inc(dist_f, 1)
            dve.tensor_scalar(dist[:, 512:640], dist_i[:, 512:640], 15.5, None, ALU.add).then_inc(dist_f, 1)
            dve.tensor_copy(dist[:, 640:896], dist_i[:, 640:896]).then_inc(dist_f, 1)
            for k in range(KC):
                dve.wait_ge(x_in[k // 2], 16)
                dve.wait_ge(x_hi0, k + 1)
                dve.tensor_tensor(x_lo[:, k, :], x[:, k, :], x_hi[:, k, :].bitcast(F32),
                                  ALU.subtract).then_inc(x_ready[0], 1)

            def up(st):
                z = st.sem
                if st.part == 0:
                    dve.sem_inc(stages[st.id + 1].sem["free"], 2)

                def hid(base, i, p, q):
                    dve.wait_ge(z["gated"], st.h0 + p + 1)
                    dve.wait_ge(slab_done, base + 2 + SLOTS * i)
                    if st.part or q >= 2:
                        dve.wait_ge(z["hhi"], st.h0 + p - 1)
                        dve.wait_ge(z["hlo"], st.h0 + p - 1)
                    dve.scalar_tensor_tensor(out=hidden[q % 2], in0=gated[q % 2], scalar=0.5,
                                             in1=bank[2 * (q % 2) + 1][:], op0=ALU.mult,
                                             op1=ALU.mult).then_inc(z["hidden"], 1)

                def lo(p, q):
                    dve.wait_ge(z["hhi"], st.h0 + p + 1)
                    dve.tensor_tensor(h_lo[:, bass.ds(p, 1), :].rearrange("p a t -> p (a t)"), hidden[q % 2],
                                      h_hi[:, bass.ds(p, 1), :].rearrange("p a t -> p (a t)").bitcast(F32),
                                      ALU.subtract).then_inc(z["hlo"], 1)

                lead = 2 - st.nf % 2
                for p in range(lead):
                    hid(st.s0 + 2 * p, 0, p, p)
                    if p:
                        lo(p - 1, p - 1)
                with dve.Fori(0, (st.nf - lead) // 2) as i:
                    for k in range(2):
                        q = lead + k
                        hid(st.s0 + 2 * q, i, q + 2 * i, q)
                        lo(q - 1 + 2 * i, q - 1)
                lo(st.nf - 1, st.nf - 1)

            def out(st):
                z = st.sem
                if st.of != "ffn":
                    dve.sem_inc(z["free"], 2)
                if st.first and st.ln:
                    dve.wait_ge(ln["xf"], KC * st.ln)
                if st.last:
                    dve.memset(ysum, 0.0).then_inc(ln["sum"], 1)
                with dve.Fori(0, 2) as i:
                    for k in range(4):
                        j = k + 4 * i
                        xj = x[:, bass.ds(j, 1), :].rearrange("p a t -> p (a t)")
                        dve.wait_ge(slab_done, st.s0 + k + 1 + SLOTS * i)
                        if st.first:
                            dve.scalar_tensor_tensor(out=xj, in0=xj, scalar=ALPHA, in1=bank[B_OUT + k % 2][:],
                                                     op0=ALU.mult, op1=ALU.add).then_inc(z["free"], 1)
                        else:
                            dve.tensor_tensor(xj, xj, bank[B_OUT + k % 2][:], ALU.add).then_inc(z["free"], 1)
                        if st.last:
                            dve.wait_ge(z["free"], KC * st.part + 3 + j)
                            dve.wait_ge(ln["sum"], (KC + 1) * st.ln + 1 + j)
                            dve.tensor_tensor(ysum, ysum, xj, ALU.add).then_inc(ln["sum"], 1)
                if st.last:
                    norm(st)

            def norm(st):
                c0 = KC * st.ln
                dve.wait_ge(ln["mu"], st.ln + 1)
                for j in range(KC):
                    dve.tensor_tensor(x[:, j, :], x[:, j, :], bank[B_MU][:], ALU.subtract).then_inc(ln["dev"], 1)
                dve.wait_ge(ln["std"], st.ln + 1)
                dve.reciprocal(rstd, std).then_inc(ln["rstd"], 1)
                dve.wait_ge(ln["rstd"], st.ln + 1)
                dve.wait_ge(ln["sq"], c0 + KC)
                if st.ln == 0:
                    dve.wait_ge(consts_in, 48)

                def lo(j):
                    dve.wait_ge(ln["hi"], c0 + j + 1)
                    dve.wait_ge(ln["norm"], c0 + j + 1)
                    dve.scalar_tensor_tensor(out=x_lo[:, j, :], in0=x[:, j, :], scalar=lnb[:, st.ln, j:j + 1],
                                             in1=x_hi[:, j, :].bitcast(F32), op0=ALU.add,
                                             op1=ALU.subtract).then_inc(x_ready[st.ln + 1], 1)

                for j in range(KC):
                    dve.scalar_tensor_tensor(out=x[:, j, :], in0=x[:, j, :], scalar=lng[:, st.ln, j:j + 1],
                                             in1=rstd, op0=ALU.mult, op1=ALU.mult).then_inc(ln["norm"], 1)
                    if j and st is not final:
                        lo(j - 1)
                if st is not final:
                    lo(KC - 1)

            def memory(st):
                if st.h0 < KC:
                    return
                for m in range(st.n // 2):
                    c = (st.h0 - KC + 2 * m) * P
                    dve.wait_ge(mem_v_tr, fill_banks(st, True) + m + 1)
                    dve.tensor_copy(memv[:, :, c:c + 2 * P].rearrange("p i (s d) -> p i s d", s=2),
                                    bank[FILL_BANKS[m]][:].rearrange("p (s i d) -> p i s d", s=2, i=MT)
                                    ).then_inc(mem_v_evac, 1)

            def kv(st):
                z = st.sem

                def values():
                    for n in range(2):
                        dve.wait_ge(z["tr"], n + 1)
                        dve.tensor_copy(vals[:, n, :, :].rearrange("p i d -> p (i d)"),
                                        bank[6 + n][:]).then_inc(z["devac"], 1)

                if st.kind == "kv_swa":
                    values()
                else:
                    dve.wait_ge(cmp_in, 96)
                    for n in range(2):
                        dve.wait_ge(z["aevac"], 1 + n)
                        src = keysT[:, 2 + n, :]
                        toks = bass.AP(src.tensor, src.offset, [list(src.ap[0]), [1, CL], [16, NCMP]])
                        dve.tensor_tensor(cblk[n], toks, cpos[:, n, :, None].to_broadcast([P, CL, NCMP]),
                                          ALU.add).then_inc(z["blkk"], 1)
                    values()
                    dve.wait_ge(z["gexp"], 1)
                    dve.tensor_scalar(gates[:], gates[:], 1.0, None, ALU.add).then_inc(z["gadd"], 1)
                    dve.wait_ge(z["gadd"], 1)
                    dve.reciprocal(gates[:], gates[:]).then_inc(z["gate"], 1)

            def attention(st):
                z = st.sem
                kind = st.kind[4:]
                T = attention_units(kind)
                nslab = 2 if kind == "x" else 1
                otok = otok_mem if kind == "x" else otok_mix
                links = [0]
                per_turn = {"swa": 2 * T.ng, "x": T.ng, "nsa": 0}[kind]
                if kind == "nsa":
                    per_turn = sum(6 if g.br == "cmp" else 3 for g in T.groups)

                def link(ins, i):
                    links[0] += 1
                    ins.then_inc(z["chain"], 1)
                    dve.wait_ge(z["chain"], links[0] + per_turn * i)

                def add(u, i):
                    dve.wait_ge(z["s"], u.u + 1 + T.n * i)
                    slot = 4 * (u.g % 4) + (0 if kind == "x" else u.i)
                    src = bank[B_S + u.u % 2]
                    if kind == "x":
                        if u.u >= 4:
                            dve.wait_ge(z["p"], u.u - 3 + T.n * i)
                        dve.reduce_max(rowmax[:, slot:slot + 1], src[:, 0:MEM], AX.X).then_inc(z["add"], 1)
                        dve.wait_ge(z["add"], u.u + 1 + T.n * i)
                        dve.tensor_scalar(negm[:, slot:slot + 1], rowmax[:, slot:slot + 1], -1.0, None,
                                          ALU.mult).then_inc(z["nm"], 1)
                        return
                    dve.wait_ge(z["bias"], u.head + 1 + T.heads * i)
                    if u.u >= 2:
                        dve.wait_ge(z["p"], u.u - 1 + T.n * i)
                    bias = biasb[u.head % 2]
                    if u.br == "cmp":
                        def blocks(t):
                            return t.rearrange("p (i n) -> p i n", i=NT)[:, :, 0:NCMP]

                        s3 = blocks(sS[u.u % 2][:, 0:P])
                        m = cmpmax
                        link(dve.tensor_tensor(s3, blocks(src[:, 0:P]), blocks(bias[:, 512:640]), ALU.add), i)
                        link(dve.tensor_reduce(m, s3, AX.X, ALU.max), i)
                        link(dve.tensor_scalar(m, m, -1.0e29, None, ALU.max), i)
                        dve.tensor_tensor(s3, s3, m[:, :, None].to_broadcast([P, NT, NCMP]),
                                          ALU.subtract).then_inc(z["nm"], 1)
                        dve.sem_inc(z["add"], 1)
                        return
                    w = P * len(u.keys)
                    b0 = (SEQ if kind == "nsa" else 256) - w
                    dve.sem_inc(cleared, 1)
                    dve.tensor_tensor_reduce(sS[u.u % 2][:, 0:w], src[:, 0:w], bias[:, b0:b0 + w], 1.0, -3.0e38,
                                             ALU.add, ALU.max, rowmax[:, slot:slot + 1]).then_inc(z["add"], 1)
                    dve.wait_ge(z["add"], u.u + 1 + T.n * i)
                    if kind == "swa":
                        dve.tensor_scalar(negm[:, slot:slot + 1], rowmax[:, slot:slot + 1],
                                          sinks[:, bass.ds(u.head + T.heads * i, 1)], -1.0,
                                          ALU.max, ALU.mult).then_inc(z["nm"], 1)
                    else:
                        dve.tensor_scalar(negm[:, slot:slot + 1], rowmax[:, slot:slot + 1], -1.0, None,
                                          ALU.mult).then_inc(z["nm"], 1)

                def cmp_sum(u, i):
                    dve.wait_ge(z["p"], u.u + 1 + T.n * i)
                    slot = 4 * (u.g % 8)
                    p3 = prob[u.u % 3][:, 0:P].rearrange("p (i n) -> p i n", i=NT)
                    dve.tensor_reduce(sums[:, slot:slot + 4], p3[:, :, 0:NCMP], AX.X, ALU.add).then_inc(z["csum"], 1)

                def finish(g, i):
                    slot = 4 * (g.g % 8)
                    src = bank[B_PV + g.g % 2]
                    dve.wait_ge(z["p"], g.last + 1 + T.n * i)
                    if kind == "x":
                        u = T.units[g.first]
                        r = rinv[:, g.g % 2:g.g % 2 + 1]
                        if g.g >= 2:
                            dve.wait_ge(z["fin"], g.g - 1 + T.ng * i)
                        link(dve.reciprocal(r, sums[:, slot:slot + 1]), i)
                        dve.wait_ge(z["pv"], u.u + 1 + T.n * i)
                        if u.first and g.b >= 2:
                            dve.wait_ge(z["ot"], 2 * (g.b - 1) + SLOTS * i)
                        dst = otok[g.b % 2].rearrange("p (i d) -> p i d", i=NT)[:, u.i, :]
                        dve.tensor_scalar(dst, src[:, 0:256], r, None, ALU.mult).then_inc(z["fin"], 1)
                        return
                    dst = otok[g.b % 2][:, 0:512].rearrange("p (i h d) -> p i h d", i=NT, h=2)[:, :, g.half, :]
                    s3 = src[:, 0:256].rearrange("p (i d) -> p i d", i=NT)
                    if kind == "swa":
                        dve.wait_ge(z["sink"], g.g + 1 + T.ng * i)
                        link(dve.tensor_tensor(tot, sums[:, slot:slot + 4], sinkexp[:, 4 * (g.g % 4):4 * (g.g % 4) + 4], ALU.add), i)
                        link(dve.reciprocal(rinv, tot), i)
                        r = rinv
                    else:
                        br = ("cmp", "sel", "win").index(g.br)
                        if br == 0:
                            n = sum(v.br == "cmp" for v in T.groups[:g.g + 1])
                            dve.wait_ge(z["csum"], n + 8 * i)
                            link(dve.tensor_scalar(tot, sums[:, slot:slot + 4], 1.0e-30, None, ALU.max), i)
                            link(dve.reciprocal(rinv, tot), i)
                        else:
                            link(dve.reciprocal(rinv, sums[:, slot:slot + 4]), i)
                        col = bass.ds(16 * br + g.head + T.heads * i, 1)
                        gt = gates[:, :, col].rearrange("p i a -> p (i a)")
                        link(dve.tensor_tensor(rgate, rinv, gt, ALU.mult), i)
                        r = rgate
                    dve.wait_ge(z["pv"], g.last + 1 + T.n * i)
                    if g.b >= 2 and g.first == T.blocks[g.b].first:
                        dve.wait_ge(z["ot"], g.b - 1 + SLOTS * i)
                    rb = r[:, :, None].to_broadcast([P, NT, 64])
                    if g.br in ("swa", "cmp"):
                        dve.tensor_tensor(dst, s3, rb, ALU.mult).then_inc(z["fin"], 1)
                    else:
                        t3 = otmp.rearrange("p (i d) -> p i d", i=NT)
                        link(dve.tensor_tensor(t3, s3, rb, ALU.mult), i)
                        dve.wait_ge(z["fin"], g.g + T.ng * i)
                        dve.tensor_tensor(dst, dst, t3, ALU.add).then_inc(z["fin"], 1)

                def out_lo(b, n, i):
                    c = nslab * b.b + n
                    dve.wait_ge(z["ohi"], c + 1 + SLOTS * i)
                    at = bass.ds(c + SLOTS * i, 1)
                    dve.tensor_tensor(h_lo[:, at, :].rearrange("p a t -> p (a t)"), bank[B_OT][:],
                                      h_hi[:, at, :].rearrange("p a t -> p (a t)").bitcast(F32),
                                      ALU.subtract).then_inc(z["olo"], 1)

                with dve.Fori(0, SLOTS * 2 // (T.nb * nslab)) as i:
                    for t in range(T.n + 9):
                        if t < T.n:
                            add(T.units[t], i)
                        if 1 <= t <= T.n and T.units[t - 1].br == "cmp":
                            cmp_sum(T.units[t - 1], i)
                        for g in T.groups:
                            if t == g.last + 4:
                                finish(g, i)
                        for b in T.blocks:
                            for n in range(nslab):
                                if t == b.last + 7 + 2 * n:
                                    out_lo(b, n, i)
                    assert links[0] == per_turn, (links, per_turn)

            for st in stages:
                if st.kind == "up":
                    up(st)
                elif st.kind == "out":
                    out(st)
                elif st.kind == "mem":
                    memory(st)
                elif st.kind.startswith("kv"):
                    kv(st)
                else:
                    attention(st)
                if st.id == 1:
                    dve.wait_ge(mem_rounded, 1)
                    dve.tensor_tensor(mem_lo, mem_raw, mem_hi.bitcast(F32), ALU.subtract).then_inc(mem_split, 1)

        @block.tensor
        def _(pe):
            def slab_ready(base, i):
                pe.wait_ge(hi_ready, base + 1 + SLOTS * i)
                pe.wait_ge(lo_ready, base + 1 + SLOTS * i)

            def product(base, dst, m_hi, m_lo, n, chunk_wait=None):
                slot = base % SLOTS
                for k in range(n):
                    if chunk_wait is not None:
                        pe.wait_ge(chunk_wait[0], chunk_wait[1] + k + 1)
                    w = slice(k * P, (k + 1) * P)
                    pe.matmul(dst, w_hi[slot][:, w], m_hi[:, k, :], start=k == 0, stop=False)
                    pe.matmul(dst, w_hi[slot][:, w], m_lo[:, k, :], start=False, stop=False)
                    last = pe.matmul(dst, w_lo[slot][:, w], m_hi[:, k, :], start=False, stop=k == n - 1)
                last.then_inc(slab_done, 1)

            def up(st):
                z = st.sem

                def pair(base, i, p, q):
                    if q == 1 and st.part == 0:
                        memory_out(pe, st)
                    for n, used in enumerate((z["gated"], z["hidden"])):
                        slab_ready(base + n, i)
                        if st.part or q >= 2:
                            pe.wait_ge(used, st.h0 + p - 1)
                        product(base + n, bank[2 * (q % 2) + n][:], x_hi, x_lo, KC,
                                (x_ready[st.x], 0) if q == 0 and n == 0 and st.part == 0 else None)

                lead = 2 - st.nf % 2
                for p in range(lead):
                    pair(st.s0 + 2 * p, 0, p, p)
                with pe.Fori(0, (st.nf - lead) // 2) as i:
                    for k in range(2):
                        pair(st.s0 + 2 * (lead + k), i, lead + k + 2 * i, lead + k)

            def out(st):
                z = st.sem
                chunks_in = (prior(st).sem["hlo"], st.h0) if st.of == "ffn" else (prior(st).sem["olo"], 0)
                with pe.Fori(0, 2) as i:
                    for k in range(4):
                        slab_ready(st.s0 + k, i)
                        pe.wait_ge(z["free"], KC * st.part + k + 1 + 4 * i)
                        product(st.s0 + k, bank[B_OUT + k % 2][:], h_hi, h_lo, st.nf, chunks_in if k == 0 else None)
                if st.last:
                    early = MEM_FILL.get(st.ln, (0, 0, 0))[2] == KC
                    if early:
                        memory_slabs(stages[st.id + 1], 0, 1)
                    pe.wait_ge(pool_set, 3 + 2 * HEADS + 1)
                    pe.wait_ge(ln["sum"], (KC + 1) * (st.ln + 1))
                    pe.matmul(bank[B_MU][:], ones[:], ysum, start=True, stop=True).then_inc(ln["mu"], 1)
                    if early:
                        memory_slabs(stages[st.id + 1], 1, 2)
                    for j in range(KC):
                        pe.wait_ge(ln["sq"], KC * st.ln + j + 1)
                        pe.matmul(bank[B_VAR][:], ones[:], square[j % 4], start=j == 0,
                                  stop=j == KC - 1).then_inc(ln["var"], 1)

            def transpose_bank(dst, src):
                for k in range(4):
                    block = slice(k * P, (k + 1) * P)
                    last = pe.transpose(dst[:, block], src[:, block], ident[:])
                return last

            def memory_slabs(st, start, stop):
                if st.ln == 0 and start == 0:
                    pe.wait_ge(mem_split, 1)
                for n in range(start, stop):
                    slab_ready(st.s0 + n, 0)
                    product(st.s0 + n, bank[FILL_BANKS[n // 2]][:, MEM * (n % 2):MEM * (n % 2 + 1)], mem_hi, mem_lo, KC)
                    if st.h0 >= KC and n >= 5 and n % 2 == 1:
                        memory_values(st, (n - 5) // 2)

            def memory_values(st, m):
                pe.wait_ge(mem_v_feat, fill_banks(st, True) + m + 1)
                transpose_bank(bank[FILL_BANKS[m]], feat[m]).then_inc(mem_v_tr, 1)

            def memory(st):
                memory_slabs(st, 2 if st.n == KC else 0, st.n)
                if st.h0 >= KC:
                    for m in range(st.n // 2 - 2, st.n // 2):
                        memory_values(st, m)

            def kv(st):
                z = st.sem
                what = kv_slabs(st.kind[3:])
                turned = [n for n, w in enumerate(what) if w[0] != "k"]

                def turn(n):
                    pe.wait_ge(z["aevac"], n + 1)
                    src = (feat if st.kind == "kv_swa" else feat_nsa)[what[n][1]]
                    transpose_bank(bank[(6, 7, 3)[turned.index(n)]], src).then_inc(z["tr"], 1)

                for n in range(st.n):
                    slab_ready(st.s0 + n, 0)
                    if n >= 4:
                        pe.wait_ge(z["aevac"], n - 3)
                    if n == 2:
                        memory_out(pe, st)
                    product(st.s0 + n, bank[n % 4][:], x_hi, x_lo, KC, (x_ready[st.x], 0) if n == 0 else None)
                    if n - 2 in turned:
                        turn(n - 2)
                if st.kind == "kv_nsa":
                    for n in range(2):
                        pe.wait_ge(z["blkk"], n + 1)
                        for half in range(2):
                            r = slice(64 * half, 64 * half + 64)
                            for l in range(CL):
                                last = pe.matmul(bank[4 + n][r, 0:NCMP], cw1[r, n, l, :], cblk[n][r, l, :],
                                                 start=l == 0, stop=l == CL - 1)
                        last.then_inc(z["c1"], 1)
                    pe.wait_ge(z["c1g"], 1)
                    pe.wait_ge(z["devac"], 2)
                    for half in range(2):
                        r = slice(64 * half, 64 * half + 64)
                        last = pe.matmul(bank[6][r, 0:NCMP], cw2[r, 0, :], ch1[0][r, :], start=True, stop=True)
                    last.then_inc(z["c2"], 1)
                    pe.wait_ge(z["c1g"], 2)
                    for half in range(2):
                        r = slice(64 * half, 64 * half + 64)
                        last = pe.matmul(bank[7 - 4 * half][0:NCMP, 0:64], ch1[1][r, :], cw2[r, 1, :],
                                         start=True, stop=True)
                    last.then_inc(z["c2"], 1)

            def attention(st):
                z = st.sem
                kind = st.kind[4:]
                T = attention_units(kind)
                nslab = 2 if kind == "x" else 1
                qs, otok = (qs_mem, otok_mem) if kind == "x" else (qs_mix, otok_mix)

                def q_block(b, i):
                    for n in range(nslab):
                        c = nslab * b.b + n
                        slab_ready(st.s0 + c, i)
                        if c:
                            pe.wait_ge(z["q"], c + SLOTS * i)
                        product(st.s0 + c, bank[0][:], x_hi, x_lo, KC,
                                (x_ready[st.x], 0) if kind == "x" and c == 0 else None)

                def q_chunk(b, k, i):
                    slot = (st.s0 + b.b) % SLOTS
                    if k == 0:
                        slab_ready(st.s0 + b.b, i)
                        pe.wait_ge(z["q"], b.b + SLOTS * i)
                    w = slice(k * P, (k + 1) * P)
                    pe.matmul(bank[0][:], w_hi[slot][:, w], x_hi[:, k, :], start=k == 0, stop=False)
                    pe.matmul(bank[0][:], w_hi[slot][:, w], x_lo[:, k, :], start=False, stop=False)
                    last = pe.matmul(bank[0][:], w_lo[slot][:, w], x_hi[:, k, :], start=False, stop=k == KC - 1)
                    if k == KC - 1:
                        last.then_inc(slab_done, 1)

                def scores(u, i):
                    if kind == "x" and u.u == 0:
                        memory_out(pe, st)
                    if u.u == T.blocks[u.b].first:
                        pe.wait_ge(z["q"], nslab * (u.b + 1) + SLOTS * i)
                    if u.u >= 2:
                        pe.wait_ge(z["p"] if kind == "x" else z["add"], u.u - 1 + T.n * i)
                    dst = bank[B_S + u.u % 2]
                    q = qs[u.b % 2]
                    r = slice(64 * u.half, 64 * u.half + 64)
                    if u.br == "cmp":
                        for n in range(NT):
                            last = pe.matmul(dst[:, 32 * n:32 * n + NCMP], q[r, 0, n * P:(n + 1) * P],
                                             kcmpT[r, :], start=True, stop=True)
                    elif kind == "x":
                        for n in range(2):
                            last = pe.matmul(dst[:, 0:MEM], q[:, n, u.i * P:(u.i + 1) * P],
                                             memkT[:, bass.ds(2 * u.b + n + 4 * i, 1), :].rearrange("p a m -> p (a m)"),
                                             start=n == 0, stop=n == 1)
                    else:
                        kt = {"sel": 0, "win": 1, "swa": u.b % 2}[u.br]
                        last = pe.matmul(dst[:, 0:P * len(u.keys)], q[r, 0, u.i * P:(u.i + 1) * P],
                                         keysT[r, kt, u.keys[0] * P:(u.keys[-1] + 1) * P], start=True, stop=True)
                    last.then_inc(z["s"], 1)

                def transposes(u, i):
                    pe.wait_ge(z["p"], u.u + 1 + T.n * i)
                    if u.u >= 2:
                        pe.wait_ge(z["pt"], u.u - 1 + T.n * i)
                    dst, src = bank[B_T + u.u % 2], prob[u.u % 3]
                    if u.br == "cmp":
                        for n in range(NT):
                            last = pe.transpose(dst[0:NCMP, n * P:(n + 1) * P], src[:, 32 * n:32 * n + NCMP], ident[:])
                    else:
                        for n in range(len(u.keys)):
                            last = pe.transpose(dst[:, n * P:(n + 1) * P], src[:, n * P:(n + 1) * P], ident[:])
                    last.then_inc(z["t"], 1)

                def values(u, i):
                    pe.wait_ge(z["pt"], u.u + 1 + T.n * i)
                    if u.first or kind == "x":
                        if u.g >= 2:
                            pe.wait_ge(z["fin"], u.g - 1 + T.ng * i)
                    dst, src = bank[B_PV + u.g % 2], probT[u.u % 2]
                    c = slice(64 * u.half, 64 * u.half + 64)
                    if u.br == "cmp":
                        for n in range(NT):
                            last = pe.matmul(dst[:, 64 * n:64 * n + 64], src[0:NCMP, n * P:(n + 1) * P], vcmp[:, c],
                                             start=True, stop=True)
                    elif kind == "x":
                        for n in range(MT):
                            last = pe.matmul(dst[:, 0:256], src[:, n * P:(n + 1) * P],
                                             memv[:, n, bass.ds(256 * u.b + 512 * i, 256)], start=n == 0, stop=n == MT - 1)
                    else:
                        v = {"sel": 0, "win": 1, "swa": u.b % 2}[u.br]
                        for n, key in enumerate(u.keys):
                            last = pe.matmul(dst[:, 64 * u.i:64 * u.i + 64], src[:, n * P:(n + 1) * P],
                                             vals[:, v, key, c], start=n == 0, stop=n == len(u.keys) - 1)
                    last.then_inc(z["pv"], 1)

                def out_transpose(b, n, i):
                    if n == 0:
                        pe.wait_ge(z["fin"], b.groups + T.ng * i)
                    c = nslab * b.b + n
                    if c:
                        pe.wait_ge(z["olo"], c + SLOTS * i)
                    for k in range(NT):
                        width = 256 if kind == "x" else P
                        last = pe.transpose(bank[B_OT][:, k * P:(k + 1) * P],
                                            otok[b.b % 2][:, width * k + n * P:width * k + (n + 1) * P], ident[:])
                    last.then_inc(z["ot"], 1)

                before = prior(st)
                if kind != "x":
                    pe.wait_ge(before.sem["aevac"], before.n)
                    pe.wait_ge(before.sem["devac"], 2)
                if kind == "nsa":
                    pe.wait_ge(before.sem["c2e"], 3)
                    pe.wait_ge(before.sem["gate"], 1)
                with pe.Fori(0, SLOTS * 2 // (T.nb * nslab)) as i:
                    for t in range(T.n + 9):
                        for b in T.blocks:
                            if t == max(b.first - 3, 0) and (nslab == 2 or b.b == 0):
                                q_block(b, i)
                        if t < T.n:
                            scores(T.units[t], i)
                        for b in T.blocks[1:]:
                            for k in range(KC):
                                back = 2 * (KC - 1 - k) if kind == "nsa" else (KC - 1 - k) // 2
                                if nslab == 1 and t == b.first - 3 - back:
                                    q_chunk(b, k, i)
                        if 2 <= t <= T.n + 1:
                            transposes(T.units[t - 2], i)
                        if 3 <= t <= T.n + 2:
                            values(T.units[t - 3], i)
                        for b in T.blocks:
                            for n in range(nslab):
                                if t == b.last + 6 + 2 * n:
                                    out_transpose(b, n, i)

            for st in stages:
                if st.kind == "up":
                    up(st)
                elif st.kind == "out":
                    out(st)
                elif st.kind == "mem":
                    memory(st)
                elif st.kind.startswith("kv"):
                    kv(st)
                else:
                    attention(st)


def slabs(w):
    k, n = w.shape
    return w.reshape(k // P, P, n // P, P).transpose(2, 1, 0, 3).reshape(n // P, P, k)


def lay_out(a):
    w8, w7 = [], []
    mem_slabs = [slabs(w) for w in a["xattn_w_kv"]]

    def memory(ln):
        if ln in MEM_FILL:
            layer, c0, n = MEM_FILL[ln]
            w8.append(mem_slabs[layer][c0:c0 + n])

    def ffn(i, gate, up, down):
        g, u = slabs(a[gate][i]), slabs(a[up][i])
        at = 0
        for nf in FPARTS:
            w8.append(np.stack([g[at:at + nf], u[at:at + nf]], 1).reshape(2 * nf, P, D))
            d = slabs(a[down][i][at * P:(at + nf) * P])
            (w8 if nf == 8 else w7).append(d)
            at += nf

    for i in range(DEPTH):
        ffn(i, "ffn1_w_gate", "ffn1_w_up", "ffn1_w_down")
        memory(4 * i)
        kind = "swa" if i == 0 else "nsa"
        w_in, w_out = a[kind + "_w_in"][0], a[kind + "_w_out"][0]
        heads = [h for pair in head_pairs(kind) for h in pair]
        cols = [w_in[:, 64 * h:64 * h + 64] for h in heads]
        rest = w_in[:, D:]
        if kind == "swa":
            w8.append(slabs(rest)[[2, 3, 0, 1]])
        else:
            kc, vc, ks, vs, kw, vw = (rest[:, P * n:P * n + P] for n in range(6))
            gl = rest[:, 6 * P:].reshape(D, 3, HEADS)[:, :, heads].reshape(D, 48)
            gl = np.concatenate([gl, np.zeros((D, P - 48), gl.dtype)], 1)
            w8.append(slabs(np.concatenate([kc, vc, vs, vw, gl, ks, kw], 1)))
        w8.append(slabs(np.concatenate(cols, 1)))
        w8.append(slabs(np.concatenate([w_out[64 * h:64 * h + 64] for h in heads], 0)))
        memory(4 * i + 1)
        w8.append(slabs(a["xattn_w_q"][i]))
        w8.append(slabs(a["xattn_w_o"][i]))
        memory(4 * i + 2)
        ffn(i, "ffn2_w_gate", "ffn2_w_up", "ffn2_w_down")
        memory(4 * i + 3)

    def feature_major(t, n):
        return np.ascontiguousarray(t.reshape(n, KC, P).transpose(2, 1, 0))

    swa_heads = [h for pair in head_pairs("swa") for h in pair]
    return {
        "w8": np.concatenate(w8, 0),
        "w7": np.concatenate(w7, 0),
        "x": feature_major(a["x"][0], SEQ),
        "mem": feature_major(a["mem"][0], MEM),
        "ln_g": feature_major(a["ln_g"].reshape(NLN, D), NLN).transpose(0, 2, 1),
        "ln_b": feature_major(a["ln_b"].reshape(NLN, D), NLN).transpose(0, 2, 1),
        "sinks": np.broadcast_to(a["swa_sinks"][0][swa_heads], (P, HEADS)),
        "cmp_pos": a["nsa_cmp_pos"][0].transpose(2, 0, 1),
        "cmp_w1": a["nsa_cmp_w1"][0].transpose(2, 0, 1, 3),
        "cmp_w2": a["nsa_cmp_w2"][0].transpose(1, 0, 2),
    }


def kernel(**inputs):
    import concourse.bacc as bacc
    from concourse.bass_utils import run_bass_kernel_spmd

    arrays = {k: np.ascontiguousarray(v) for k, v in lay_out({k: np.asarray(v) for k, v in inputs.items()}).items()}
    nc = bacc.Bacc("TRN2", target_bir_lowering=False, num_devices=1)
    io = {k: nc.dram_tensor(k + "_dram", v.shape, mybir.dt.from_np(v.dtype), kind="ExternalInput").ap()
          for k, v in arrays.items()}
    io["out"] = nc.dram_tensor("out_dram", (P, KC, SEQ), F32, kind="ExternalOutput").ap()
    build(nc, io)
    r = run_bass_kernel_spmd(nc, [{k + "_dram": v for k, v in arrays.items()}], core_ids=[0])
    return r.results[0]["out_dram"].transpose(2, 1, 0).reshape(1, SEQ, D)
```
